# Optimizing a Trainium2 kernel written in Bass

```python
import math
import jax, jax.numpy as jnp
from jax import lax
import numpy as np

D_MODEL = 1024
BATCH = 1
SEQ = 512
DEPTH = 1

HEAD_DIM = 64
D_MIX = D_MODEL
NSA_HEADS = 8
NSA_KV_HEADS = 2
NSA_Q_PER_KV = NSA_HEADS // NSA_KV_HEADS
DIL_HEADS = 8
W_NSA = NSA_HEADS * HEAD_DIM
W_KV = NSA_KV_HEADS * HEAD_DIM
W_DIL = DIL_HEADS * HEAD_DIM
CMP_LEN = 32
CMP_STRIDE = 16
CMP_HIDDEN = 256
SEL_BLOCK = 64
SEL_TOP_N = 16
SWA_WINDOW = 512
DIL_PATTERNS = ((128, 1), (512, 4), (2048, 16))
BLOCK = 128
ROPE_THETA = 500000.0
ROPE_DIMS = HEAD_DIM // 4
RMS_EPS = 1e-6
NEG_INF = -1e30
FORCE_SCORE = 1e4
IN_SPLITS = (W_NSA,
             W_KV, W_KV,
             W_KV, W_KV,
             W_KV, W_KV,
             3 * NSA_HEADS,
             W_NSA,
             W_DIL, W_DIL, W_DIL,
             W_DIL)
D_IN = sum(IN_SPLITS)

kernel_name = "hymba_nsa_dilated_hybrid"

def rmsnorm(x, g):
    xf = x.astype(jnp.float32)
    y = xf * lax.rsqrt(jnp.mean(xf * xf, axis=-1, keepdims=True) + RMS_EPS)
    return (y * g.astype(jnp.float32)).astype(x.dtype)

def rope_tables(positions):
    inv = 1.0 / (ROPE_THETA ** (jnp.arange(0, ROPE_DIMS, 2, dtype=jnp.float32) / ROPE_DIMS))
    ang = positions.astype(jnp.float32)[..., None] * inv
    return jnp.cos(ang), jnp.sin(ang)

def apply_rope(x, cos, sin):
    shape = (cos.shape[0],) + (1,) * (x.ndim - 3) + cos.shape[1:]
    c = cos.reshape(shape)
    s = sin.reshape(shape)
    half = ROPE_DIMS // 2
    xf = x.astype(jnp.float32)
    x1 = xf[..., :half]
    x2 = xf[..., half:ROPE_DIMS]
    out = jnp.concatenate([x1 * c - x2 * s, x2 * c + x1 * s, xf[..., ROPE_DIMS:]], axis=-1)
    return out.astype(x.dtype)

def banded_attention(q, k, v, window):
    B, G, R, L, D = q.shape
    nblk = -(-L // BLOCK)
    Lp = nblk * BLOCK
    nprev = -(-window // BLOCK)
    qp = jnp.pad(q, ((0, 0), (0, 0), (0, 0), (0, Lp - L), (0, 0)))
    kp = jnp.pad(k, ((0, 0), (0, 0), (nprev * BLOCK, Lp - L), (0, 0)))
    vp = jnp.pad(v, ((0, 0), (0, 0), (nprev * BLOCK, Lp - L), (0, 0)))
    qb = qp.reshape(B, G, R, nblk, BLOCK, D)
    kb = kp.reshape(B, G, nprev + nblk, BLOCK, D)
    vb = vp.reshape(B, G, nprev + nblk, BLOCK, D)
    kw = jnp.concatenate([kb[:, :, j:j + nblk] for j in range(nprev + 1)], axis=3)
    vw = jnp.concatenate([vb[:, :, j:j + nblk] for j in range(nprev + 1)], axis=3)
    i = jnp.arange(BLOCK)[:, None]
    c = jnp.arange((nprev + 1) * BLOCK)[None, :]
    dist = nprev * BLOCK + i - c
    kabs = (jnp.arange(nblk)[:, None, None] - nprev) * BLOCK + c[None]
    mask = (dist >= 0)[None] & (dist <= window)[None] & (kabs >= 0)
    s = jnp.einsum('bgrnqd,bgnkd->bgrnqk', qb, kw).astype(jnp.float32) * (HEAD_DIM ** -0.5)
    s = jnp.where(mask, s, NEG_INF)
    m = jnp.max(s, axis=-1, keepdims=True)
    e = jnp.exp(s - m)
    den = jnp.sum(e, axis=-1, keepdims=True)
    p = (e / den).astype(v.dtype)
    out = jnp.einsum('bgrnqk,bgnkd->bgrnqd', p, vw).reshape(B, G, R, Lp, D)[:, :, :, :L]
    lse = (m[..., 0] + jnp.log(den[..., 0])).reshape(B, G, R, Lp)[..., :L]
    return out, lse

def compress_blocks(k, pos_emb, w1, w2):
    B, G, S, D = k.shape
    n_cmp = (S - CMP_LEN) // CMP_STRIDE + 1
    idx = jnp.arange(n_cmp)[:, None] * CMP_STRIDE + jnp.arange(CMP_LEN)[None, :]
    blocks = k[:, :, idx] + pos_emb
    flat = blocks.reshape(B, G, n_cmp, CMP_LEN * D)
    return jax.nn.silu(flat @ w1) @ w2

def nsa_compressed_and_selected(q, k_cmp, v_cmp, k_slc, v_slc):
    B, G, R, S, D = q.shape
    n_cmp = k_cmp.shape[2]
    n_sel = S // SEL_BLOCK
    top_n = min(SEL_TOP_N, n_sel)
    scale = HEAD_DIM ** -0.5
    cmp_end = jnp.arange(n_cmp) * CMP_STRIDE + CMP_LEN - 1
    ratio = SEL_BLOCK // CMP_STRIDE
    offs = np.array([m - n for m in range(ratio) for n in range(CMP_LEN // CMP_STRIDE)], dtype=np.int32)
    cidx = jnp.arange(n_sel)[:, None] * ratio + offs[None, :]
    cvalid = (cidx >= 0) & (cidx < n_cmp)
    cidx = jnp.clip(cidx, 0, n_cmp - 1)
    kb = k_slc.reshape(B, G, n_sel, SEL_BLOCK, D)
    vb = v_slc.reshape(B, G, n_sel, SEL_BLOCK, D)
    bi = jnp.arange(B)[:, None, None, None]
    gi = jnp.arange(G)[None, :, None, None]
    blk = jnp.arange(n_sel)

    def one_block(b):
        t = b * BLOCK + jnp.arange(BLOCK)
        qb = lax.dynamic_slice_in_dim(q, b * BLOCK, BLOCK, axis=3)
        s = jnp.einsum('bgrqd,bgcd->bgrqc', qb, k_cmp).astype(jnp.float32) * scale
        valid = cmp_end[None, :] <= t[:, None]
        s = jnp.where(valid, s, NEG_INF)
        m = jnp.max(s, axis=-1, keepdims=True)
        p = jnp.where(valid, jnp.exp(s - m), 0.0)
        p = p / jnp.maximum(jnp.sum(p, axis=-1, keepdims=True), 1e-30)
        o_cmp = jnp.einsum('bgrqc,bgcd->bgrqd', p.astype(v_cmp.dtype), v_cmp)
        imp = jnp.sum(p, axis=2)
        imp_sel = jnp.sum(jnp.where(cvalid, imp[..., cidx], 0.0), axis=-1)
        cur = t // SEL_BLOCK
        blk_valid = blk[None, :] <= cur[:, None]
        forced = (blk[None, :] == 0) | (blk[None, :] == cur[:, None]) | (blk[None, :] == cur[:, None] - 1)
        score = jnp.where(forced, FORCE_SCORE, imp_sel)
        score = jnp.where(blk_valid, score, -1.0)
        _, idx = lax.top_k(score, top_n)
        sel_ok = idx <= cur[:, None]
        ksel = kb[bi, gi, idx]
        vsel = vb[bi, gi, idx]
        s2 = jnp.einsum('bgrqd,bgqnld->bgrqnl', qb, ksel).astype(jnp.float32) * scale
        kpos = idx[..., None] * SEL_BLOCK + jnp.arange(SEL_BLOCK)
        ok = sel_ok[..., None] & (kpos <= t[:, None, None])
        s2 = jnp.where(ok[:, :, None], s2, NEG_INF)
        p2 = jax.nn.softmax(s2.reshape(B, G, R, BLOCK, top_n * SEL_BLOCK), axis=-1)
        p2 = p2.reshape(B, G, R, BLOCK, top_n, SEL_BLOCK).astype(v_slc.dtype)
        o_slc = jnp.einsum('bgrqnl,bgqnld->bgrqd', p2, vsel)
        return o_cmp, o_slc

    o_cmp, o_slc = lax.map(one_block, jnp.arange(S // BLOCK))
    o_cmp = jnp.transpose(o_cmp, (1, 2, 3, 0, 4, 5)).reshape(B, G, R, S, D)
    o_slc = jnp.transpose(o_slc, (1, 2, 3, 0, 4, 5)).reshape(B, G, R, S, D)
    return o_cmp, o_slc

def dilated_mixture(q, k, v):
    B, H, S, D = q.shape
    outs, lses = [], []
    for window, dil in DIL_PATTERNS:
        L = S // dil
        qd = q.reshape(B, H, L, dil, D).transpose(0, 1, 3, 2, 4).reshape(B, H * dil, 1, L, D)
        kd = k.reshape(B, H, L, dil, D).transpose(0, 1, 3, 2, 4).reshape(B, H * dil, L, D)
        vd = v.reshape(B, H, L, dil, D).transpose(0, 1, 3, 2, 4).reshape(B, H * dil, L, D)
        o, lse = banded_attention(qd, kd, vd, window // dil)
        outs.append(o.reshape(B, H, dil, L, D).transpose(0, 1, 3, 2, 4).reshape(B, H, S, D))
        lses.append(lse.reshape(B, H, dil, L).transpose(0, 1, 3, 2).reshape(B, H, S))
    w = jax.nn.softmax(jnp.stack(lses, axis=0), axis=0)
    o = jnp.sum(w[..., None] * jnp.stack(outs, axis=0).astype(jnp.float32), axis=0)
    return o.astype(q.dtype)

def setup_inputs(seed: int = 0) -> dict:
    key = jax.random.key(seed)
    ks = jax.random.split(key, 14)
    f32 = jnp.float32
    x = jax.random.normal(ks[0], (BATCH, SEQ, D_MODEL), f32)
    offs = jax.random.randint(ks[1], (BATCH, 1), 0, 4096, dtype=jnp.int32)
    positions = offs + jnp.arange(SEQ, dtype=jnp.int32)[None, :]
    pre_norm_g = 1.0 + 0.02 * jax.random.normal(ks[2], (DEPTH, D_MODEL), f32)
    w_in = jax.random.normal(ks[3], (DEPTH, D_MODEL, D_IN), f32) * D_MODEL ** -0.5
    cmp_k_pos = 0.1 * jax.random.normal(ks[4], (DEPTH, CMP_LEN, HEAD_DIM), f32)
    cmp_k_w1 = jax.random.normal(ks[5], (DEPTH, CMP_LEN * HEAD_DIM, CMP_HIDDEN), f32) * (CMP_LEN * HEAD_DIM) ** -0.5
    cmp_k_w2 = jax.random.normal(ks[6], (DEPTH, CMP_HIDDEN, HEAD_DIM), f32) * CMP_HIDDEN ** -0.5
    cmp_v_pos = 0.1 * jax.random.normal(ks[7], (DEPTH, CMP_LEN, HEAD_DIM), f32)
    cmp_v_w1 = jax.random.normal(ks[8], (DEPTH, CMP_LEN * HEAD_DIM, CMP_HIDDEN), f32) * (CMP_LEN * HEAD_DIM) ** -0.5
    cmp_v_w2 = jax.random.normal(ks[9], (DEPTH, CMP_HIDDEN, HEAD_DIM), f32) * CMP_HIDDEN ** -0.5
    w_out = jax.random.normal(ks[10], (DEPTH, D_MIX, D_MODEL), f32) * D_MIX ** -0.5
    post_norm_g = 1.0 + 0.02 * jax.random.normal(ks[11], (DEPTH, D_MODEL), f32)
    return {"x": x, "positions": positions, "pre_norm_g": pre_norm_g, "w_in": w_in,
            "cmp_k_pos": cmp_k_pos, "cmp_k_w1": cmp_k_w1, "cmp_k_w2": cmp_k_w2,
            "cmp_v_pos": cmp_v_pos, "cmp_v_w1": cmp_v_w1, "cmp_v_w2": cmp_v_w2,
            "w_out": w_out, "post_norm_g": post_norm_g}

def reference(x, positions, pre_norm_g, w_in, cmp_k_pos, cmp_k_w1, cmp_k_w2,
              cmp_v_pos, cmp_v_w1, cmp_v_w2, w_out, post_norm_g):
    B, S, _ = x.shape
    G, R, D = NSA_KV_HEADS, NSA_Q_PER_KV, HEAD_DIM
    cos, sin = rope_tables(positions)
    for layer in range(DEPTH):
        h = rmsnorm(x, pre_norm_g[layer])
        proj = h @ w_in[layer]
        parts, start = [], 0
        for width in IN_SPLITS:
            parts.append(proj[..., start:start + width])
            start += width
        (q_a, k_cmp, v_cmp, k_slc, v_slc, k_win, v_win, gate_a, z_a,
         q_b, k_b, v_b, z_b) = parts

        qa = apply_rope(q_a.reshape(B, S, G, R, D).transpose(0, 2, 3, 1, 4), cos, sin)
        kv = lambda t: t.reshape(B, S, G, D).transpose(0, 2, 1, 3)
        kc = compress_blocks(apply_rope(kv(k_cmp), cos, sin), cmp_k_pos[layer], cmp_k_w1[layer], cmp_k_w2[layer])
        vc = compress_blocks(kv(v_cmp), cmp_v_pos[layer], cmp_v_w1[layer], cmp_v_w2[layer])
        o_cmp, o_slc = nsa_compressed_and_selected(qa, kc, vc, apply_rope(kv(k_slc), cos, sin), kv(v_slc))
        o_win, _ = banded_attention(qa, apply_rope(kv(k_win), cos, sin), kv(v_win), SWA_WINDOW - 1)
        g = jax.nn.sigmoid(gate_a.astype(jnp.float32)).reshape(B, S, 3, G, R).transpose(2, 0, 3, 4, 1)[..., None]
        o_a = (g[0] * o_cmp + g[1] * o_slc + g[2] * o_win).astype(x.dtype)
        o_a = o_a.transpose(0, 3, 1, 2, 4).reshape(B, S, W_NSA)

        heads = lambda t: t.reshape(B, S, DIL_HEADS, D).transpose(0, 2, 1, 3)
        o_b = dilated_mixture(apply_rope(heads(q_b), cos, sin), apply_rope(heads(k_b), cos, sin), heads(v_b))
        o_b = o_b.transpose(0, 2, 1, 3).reshape(B, S, W_DIL)

        mixed = jnp.concatenate([o_a * jax.nn.silu(z_a), o_b * jax.nn.silu(z_b)], axis=-1)
        x = x + rmsnorm(mixed @ w_out[layer], post_norm_g[layer])
    return x


_drawn_inputs = setup_inputs


def setup_inputs(seed=0):
    import zlib

    import numpy as np

    out = dict(_drawn_inputs(seed))
    spreads = {}
    factors = {'cmp_k_pos': 6.361, 'post_norm_g': 4.002}
    for name, (base, spread) in spreads.items():
        noise = np.random.default_rng([zlib.crc32(name.encode()), seed]).standard_normal(out[name].shape)
        drawn = base * np.exp(spread * noise) if base else spread * noise
        out[name] = __import__('jax').numpy.asarray(drawn.astype(out[name].dtype))
    for name, factor in factors.items():
        out[name] = (out[name] * factor).astype(out[name].dtype)
    return out
```

```python
from contextlib import ExitStack

import numpy as np

import concourse.bass as bass
from concourse import mybir

ALU = mybir.AluOpType
ACT = mybir.ActivationFunctionType
AX = mybir.AxisListType.X
F32 = mybir.dt.float32
F32R = mybir.dt.float32r
F16 = mybir.dt.float16
BF16 = mybir.dt.bfloat16
I32 = mybir.dt.int32

P = 128
S = 512
DM = 1024
HD = 64
NT = S // P
NC = DM // P
NSA_PAIRS = 4
DIL_PAIRS = 4
PAIRS = NSA_PAIRS + DIL_PAIRS
CL, CS, CH = 32, 16, 256
NB = (S - CL) // CS + 1
CP = 32
EPS = 1e-6
SCALE = HD ** -0.5
NEG = -1e30
BIG = 3e38

COL = dict(q_a=0, k_cmp=512, v_cmp=640, k_slc=768, v_slc=896, k_win=1024, v_win=1152, gate=1280,
           z_a=1304, q_b=1816, k_b=2328, v_b=2840, z_b=3352)
NG = 24
VSG = 2 * P + NG

C_ID, C_ROT, C_INV = 0, P, 2 * P
C_CAUSAL = 2 * P + 1
C_DIL = C_CAUSAL + S
C_CADD = C_DIL + S
C_CVAL = C_CADD + NT * CP
C_END = C_CVAL + NT * CP

TWO_PI = 2 * np.pi
TP1 = 6.28125
TP2 = float(np.round((TWO_PI - TP1) * 2 ** 20) / 2 ** 20)
TP3 = float(np.float32(TWO_PI - TP1 - TP2))
ROUND = 1.5 * 2 ** 23
PI_IN = 3.1415925

ROPE, COPY, SILU = "rope", "copy", "silu"


def weight_tiles():
    tiles = []
    for name, how in (("k_cmp", ROPE), ("v_cmp", COPY), ("k_slc", ROPE), ("k_win", ROPE)):
        tiles.append(("proj", COL[name], how))
    tiles += [("w1k", j, None) for j in range(4)]
    tiles += [("w1v", j, None) for j in range(4)]
    tiles += [("pair", COL["q_a"] + HD * j, ROPE) for j in range(4)]
    tiles += [("vsg", j, None) for j in range(4)]
    tiles += [("proj", COL["q_b"] + P * j, ROPE) for j in range(4)]
    tiles += [("proj", COL["k_b"] + P * j, ROPE) for j in range(4)]
    tiles += [("vb", j, None) for j in range(4)]
    tiles += [("pair", COL["z_a"] + HD * j, SILU) for j in range(4)]
    tiles += [("proj", COL["z_b"] + P * j, SILU) for j in range(4)]
    tiles += [("out", j, None) for j in range(8)]
    return tiles


def hymba_kernel(nc, x, positions, pre_g, w_in, ck_pos, ck_w1, ck_w2, cv_pos, cv_w1, cv_w2, w_out, post_g,
                 consts, out):
    tiles = weight_tiles()
    NW = len(tiles)
    NPH = NW - 8
    proj = [r for r in range(NW) if tiles[r][0] in ("proj", "pair")]
    t_of = {r: t for t, r in enumerate(proj)}
    ropes = [r for r in proj if tiles[r][2] == ROPE]
    rho_of = {r: n for n, r in enumerate(ropes)}
    R_VSG = next(r for r in range(NW) if tiles[r][0] == "vsg")
    R_VB = next(r for r in range(NW) if tiles[r][0] == "vb")
    R_W1K, R_W1V = 4, 8

    ctx = ExitStack()
    with ctx:
        def sb(name, shape, dt=F32):
            return ctx.enter_context(nc.sbuf_tensor(name, shape, dt))

        def sem(name):
            return ctx.enter_context(nc.semaphore(name))

        def r32(ap):
            return ap.bitcast(F32R)

        cst = sb("cst", [P, C_END])
        ident = cst[:, C_ID:C_ID + P]
        rot = cst[:, C_ROT:C_ROT + P]
        inv = cst[:, C_INV:C_INV + 1]
        causal = cst[:, C_CAUSAL:C_CAUSAL + S]
        dilated = cst[:, C_DIL:C_DIL + S]
        cadd = cst[:, C_CADD:C_CADD + NT * CP].rearrange("p (t c) -> p t c", t=NT)
        cval = cst[:, C_CVAL:C_CVAL + NT * CP].rearrange("p (t c) -> p t c", t=NT)
        raw = sb("raw", [P, 4, DM])
        w_h = sb("w_h", [P, 2, DM])
        w_l = sb("w_l", [P, 2, DM])
        q_l = sb("q_l", [P, PAIRS, S])
        k_h = sb("k_h", [P, 2 + DIL_PAIRS, S])
        k_l = sb("k_l", [P, 2 + DIL_PAIRS, S])
        zreg = sb("zreg", [P, PAIRS, S])
        vreg = sb("vreg", [P, 12 * 4 * 3 * HD // 2])
        v3 = vreg[:, :].bitcast(BF16).rearrange("p (u k s d) -> p u k s d", u=12, k=NT, s=3)
        x_in = vreg[:, 0:NT * DM].rearrange("p (t n) -> p t n", t=NT)
        gpre = sb("gpre", [P, NC])
        stat = sb("stat", [P, 64])
        gates = sb("gates", [P, NT, NG])
        gw = sb("gw", [P, 12, NT, 2])
        den = sb("den", [P, 2, NT, 2])
        nmx = sb("nmx", [P, 2, NT, 2])
        rw = sb("rw", [P, 2, NT, 2])
        cden = sb("cden", [P, 3, NT * 8])

        def overlay(*specs):
            with ExitStack() as own:
                return [own.enter_context(nc.sbuf_tensor(n, [P, w], F32))[:, :] for n, w in specs]

        x_n, = overlay(("x_n", NT * DM))
        x_n = x_n.rearrange("p (t n) -> p t n", t=NT)
        q_h = sb("q_h", [P, PAIRS, S])

        h_h, h_l = (t.rearrange("p (c s) -> p c s", c=NC) for t in overlay(("h_h", NC * S), ("h_l", NC * S)))
        PW = 1280
        prob, pt_h, pt_l, mix = overlay(("prob", 4 * PW), ("pt_h", 1024), ("pt_l", 1024), ("mix", 1024))
        prob = prob.rearrange("p (u a n) -> p u a n", u=2, a=2)
        pt_h = pt_h.bitcast(F16).rearrange("p (m n) -> p m n", m=4)
        pt_l = pt_l.bitcast(F16).rearrange("p (m n) -> p m n", m=4)
        mix = mix.rearrange("p (m n) -> p m n", m=2)
        y_out, junk = overlay(("y_out", NT * DM), ("junk", DM))
        y_out = y_out.rearrange("p (t n) -> p t n", t=NT)
        sb("first_area", [P, 2 * NC * S])

        FW = 16 * 2 * NB
        fkh, fkl, fvh, fvl, _, f_tmp, kc_t, vc_t, xf, uu, tt, rr, cos_t, sin_t = overlay(
            ("fkh", FW), ("fkl", FW), ("fvh", FW), ("fvl", FW), ("gap", 4 * (1024 - FW)), ("f_tmp", 1024),
            ("kc_t", S), ("vc_t", S), ("xf", 2 * S), ("uu", 2 * S), ("tt", S), ("rr", 2 * S),
            ("cos_t", S), ("sin_t", S))
        f_h, f_l = (fkh, fvh), (fkl, fvl)
        f_tmp = f_tmp[:, 0:FW]
        xf, uu, rr = (t.rearrange("p (b s) -> p b s", b=2) for t in (xf, uu, rr))
        oc, pct, cs = overlay(("oc", 4 * S), ("pct", 4 * S), ("cs", NT * 8 * CP))
        oc = oc.rearrange("p (a s) -> p a s", a=4)
        pct = pct.rearrange("p (a s) -> p a s", a=4)
        cs = cs.rearrange("p (t h c) -> p t h c", t=NT, h=8)
        _, gpost = overlay(("gap2", 4 * S), ("gpost", DM))
        startup, = overlay(("startup", 10752))
        sb("second_area", [P, 10752])
        posi = startup[:, 0:512].bitcast(I32)
        posf = startup[:, 512:1024]
        ang = startup[:, 1024:1536]
        trn = [startup[:, 1536:2048], startup[:, 2048:2560]]
        red = [startup[:, 2560:3072], startup[:, 3072:3584]]
        xjunk = startup[:, 5632:5632 + DM]
        zf = zreg[:, :, :].rearrange("p a s -> p (a s)")
        w2k = zf[:, 0:256].rearrange("p (j n) -> p j n", j=2)
        w2v = zf[:, 256:384].rearrange("p (j n) -> p j n", j=2)
        posr = [zf[0:CL, 384 + 128 * i:512 + 128 * i] for i in range(2)]
        grow = zf[0:NC, 2112:2240]
        post = [zf[:, 640 + 32 * i:672 + 32 * i] for i in range(2)]
        h1s = [zf[0:2 * NB, 704 + 256 * i:960 + 256 * i] for i in range(2)]
        h1kt = zf[:, 1216:1216 + 4 * NB].rearrange("p (j n) -> p j n", j=2)
        h1vt = zf[:, 1344:1472].rearrange("p (j g n) -> p j g n", j=2, g=2)
        kbd_h = sb("kbd_h", [P, 2 * CP])
        kbd_l = sb("kbd_l", [P, 2 * CP])
        vbd = zf[0:2 * CP, 1856:1856 + P]

        ps = ctx.enter_context(nc.psum_tensor("ps", [P, 8, S], F32))

        x_load = [sem(f"x_load{t}") for t in range(NT)]
        c_load = sem("c_load")
        t_load = sem("t_load")
        p_load = sem("p_load")
        g_load = sem("g_load")
        k_load = sem("k_load")
        w_load = [sem(f"w_load{s}") for s in range(4)]
        w_hi, w_lo, w_used = sem("w_hi"), sem("w_lo"), sem("w_used")
        ssq, var, std, rstd, xn_done = sem("ssq"), sem("var"), sem("std"), sem("rstd"), sem("xn_done")
        angle, table = sem("angle"), sem("table")
        x_tr, h_hi, h_lo = sem("x_tr"), sem("h_hi"), sem("h_lo")
        t_evac, rotated = sem("t_evac"), sem("rotated")
        rope_mul, rope_u, rope_add, rope_hi, rope_lo = (sem("rope_mul"), sem("rope_u"), sem("rope_add"),
                                                        sem("rope_hi"), sem("rope_lo"))
        zeroed = sem("zeroed")
        pos_tr, pos_cp = sem("pos_tr"), sem("pos_cp")
        f_built, f_hid, f_lod = sem("f_built"), sem("f_hid"), sem("f_lod")
        h1_silu, h1_tr, h1_cp, c_mm, c_hi, c_lo = (sem("h1_silu"), sem("h1_tr"), sem("h1_cp"), sem("c_mm"),
                                                   sem("c_hi"), sem("c_lo"))
        v_hi, v_rest, v_mid, v_done = sem("v_hi"), sem("v_rest"), sem("v_mid"), sem("v_done")
        gate_e, gate_s = sem("gate_e"), sem("gate_s")
        cs_mm, cs_dve, cs_exp, cp_tr, cp_cp, co_mm, co_cp = (sem("cs_mm"), sem("cs_dve"), sem("cs_exp"),
                                                            sem("cp_tr"), sem("cp_cp"), sem("co_mm"),
                                                            sem("co_cp"))
        s_ready, s_masked, p_exp, w_ready = sem("s_ready"), sem("s_masked"), sem("p_exp"), sem("w_ready")
        p_rec, pn_v, pn_g = sem("p_rec"), sem("pn_v"), sem("pn_g")
        pt_ready, pt_hi, pt_lo, pv_done = sem("pt_ready"), sem("pt_hi"), sem("pt_lo"), sem("pv_done")
        o_read, mix_add, mix_z, m_hi, m_lo = (sem("o_read"), sem("mix_add"), sem("mix_z"), sem("m_hi"),
                                              sem("m_lo"))
        y_mm, y_sq, y_var, y_std, y_rstd, y_mul, y_add, y_out_s = (
            sem("y_mm"), sem("y_sq"), sem("y_var"), sem("y_std"), sem("y_rstd"), sem("y_mul"), sem("y_add"),
            sem("y_out"))
        r_load = sem("r_load")
        chain = sem("chain")

        w_in_v = w_in.rearrange("(c p) n -> p c n", p=P)
        w1_v = {"w1k": ck_w1.rearrange("(j p) n -> p j n", p=P), "w1v": cv_w1.rearrange("(j p) n -> p j n", p=P)}
        x_v = x.rearrange("b (t p) n -> p (b t) n", p=P)
        out_v = out.rearrange("b (t p) n -> p (b t) n", p=P)

        def off(qt):
            return P * qt * (qt + 1) // 2

        def width(r):
            return 2 * VSG if tiles[r][0] == "vsg" else DM

        def unit(U):
            if U < 2 * NSA_PAIRS:
                return U // 2, U % 2, 2 * (U % 2)
            i = U - 2 * NSA_PAIRS
            return NSA_PAIRS + i, 2 + i, 4 + 2 * i

        def qk_slot(n):
            if n < 3:
                return k_h[:, n - 1, :], k_l[:, n - 1, :]
            if n < 11:
                return q_h[:, n - 3, :], q_l[:, n - 3, :]
            return k_h[:, n - 9, :], k_l[:, n - 9, :]

        def mixed_after(U):
            if U < 2 * NSA_PAIRS:
                return U // 2 if U % 2 else None
            return U - NSA_PAIRS

        NU = 2 * NSA_PAIRS + DIL_PAIRS

        block = ctx.enter_context(nc.Block())

        @block.sync
        def _(sp):
            for t in range(NT):
                sp.dma_start(x_in[:, t, :], x_v[:, t, :]).then_inc(x_load[t], 16)

            def load_weights(r):
                kind, j, _ = tiles[r]
                done = w_load[r % 4]
                if r >= 4:
                    sp.wait_ge(w_lo, r - 3)
                if kind == "proj":
                    v = raw[:, r % 4, :].rearrange("p (c n) -> p c n", c=NC)
                    for h in range(2):
                        sp.dma_start(v[:, 4 * h:4 * h + 4, :], w_in_v[:, 4 * h:4 * h + 4, j:j + P]).then_inc(done, 16)
                elif kind == "pair":
                    v = raw[:, r % 4, :].rearrange("p (c n) -> p c n", c=NC)
                    for h in range(2):
                        sp.dma_start(v[:, :, HD * h:HD * h + HD],
                                     w_in_v[:, :, j + 4 * HD * h:j + 4 * HD * h + HD]).then_inc(done, 16)
                elif kind in w1_v:
                    v = raw[:, r % 4, :].rearrange("p (c n) -> p c n", c=4)
                    for h in range(2):
                        sp.dma_start(v[:, 2 * h:2 * h + 2, :],
                                     w1_v[kind][:, 4 * j + 2 * h:4 * j + 2 * h + 2, :]).then_inc(done, 16)
                elif kind == "vsg":
                    v = raw[:, r % 4, 0:2 * VSG].rearrange("p (c n) -> p c n", c=2)
                    a, b = COL["v_slc"], COL["v_win"]
                    sp.dma_start(v[:, :, 0:P], w_in_v[:, 2 * j:2 * j + 2, a:a + P]).then_inc(done, 16)
                    sp.dma_start(v[:, :, P:VSG], w_in_v[:, 2 * j:2 * j + 2, b:b + VSG - P]).then_inc(done, 16)
                elif kind == "vb":
                    for h in range(2):
                        sp.dma_start(raw[:, r % 4, S * h:S * h + S],
                                     w_in_v[:, 2 * j + h, COL["v_b"]:COL["v_b"] + S]).then_inc(done, 16)
                else:
                    for h in range(2):
                        row = HD * (j + 4 * h) if j < NSA_PAIRS else P * j + HD * h
                        sp.dma_start(raw[HD * h:HD * h + HD, r % 4, :], w_out[row:row + HD, :]).then_inc(done, 16)

            for r in range(NW):
                load_weights(r)
            sp.wait_ge(co_mm, 4)
            sp.dma_start(gpost, post_g.partition_broadcast(P)).then_inc(g_load, 16)
            sp.wait_ge(pv_done, 4 * NU)
            for t in range(NT):
                sp.dma_start(x_in[:, t, :], x_v[:, t, :]).then_inc(r_load, 16)
            for t in range(NT):
                sp.wait_ge(y_add, t + 1)
                sp.dma_start(out_v[:, t, :], y_out[:, t, :]).then_inc(y_out_s, 16)
            sp.wait_ge(y_out_s, 16 * NT)

        @block.gpsimd
        def _(pool):
            nc.gpsimd.memset(zf[:, 1344:2112], 0.0)
            nc.gpsimd.memset(kbd_h[:, :], 0.0)
            nc.gpsimd.memset(kbd_l[:, :], 0.0).then_inc(zeroed, 1)
            nc.gpsimd.memset(gw[:, 2 * NSA_PAIRS:NU, :, :], 1.0).then_inc(zeroed, 1)
            pool.wait_ge(table, 2)
            for n, r in enumerate(ropes):
                pool.wait_ge(t_evac, t_of[r] + 1)
                if n >= 2:
                    pool.wait_ge(rope_add, n - 1)
                nc.gpsimd.tensor_tensor(uu[:, n % 2, :], xf[:, n % 2, :], cos_t, ALU.mult).then_inc(rope_u, 1)
            for U in range(NU):
                for i in range(2):
                    qt = 3 - i
                    N = P * (qt + 1)
                    pool.wait_ge(w_ready, 4 * U + i + 1)
                    for a in range(2):
                        pa = prob[:, U % 2, a, off(qt):off(qt) + N]
                        last = nc.gpsimd.tensor_tensor(
                            pa, pa, rw[:, U % 2, qt, a:a + 1].to_broadcast([P, N]), ALU.mult)
                    last.then_inc(pn_g, 1)

        @block.scalar
        def _(act):
            act.dma_start(posi, positions.rearrange("b s -> (b s)").partition_broadcast(P)).then_inc(p_load, 16)
            act.dma_start(cst[:, 0:C_CAUSAL], consts[:, 0:C_CAUSAL]).then_inc(c_load, 16)
            act.dma_start(grow, pre_g.rearrange("(c p) -> c p", p=P)).then_inc(k_load, 16)
            for i, (pos, w2) in enumerate(((ck_pos, ck_w2), (cv_pos, cv_w2))):
                for h in range(2):
                    act.dma_start(posr[i][:, HD * h:HD * h + HD], pos).then_inc(k_load, 16)
            w2v_k = ck_w2.rearrange("(j p) n -> p j n", p=P)
            for h in range(2):
                act.dma_start(w2k[:, :, HD * h:HD * h + HD], w2v_k).then_inc(k_load, 16)
            act.dma_start(w2v, cv_w2.rearrange("(j p) n -> p j n", p=P)).then_inc(k_load, 16)
            act.dma_start(cst[:, C_CAUSAL:C_END], consts[:, C_CAUSAL:C_END]).then_inc(t_load, 16)

            for t in range(NT):
                act.wait_ge(x_load[t], 16)
                if t:
                    act.wait_ge(ssq, t)
                nc.scalar.activation(xjunk, x_in[:, t, :], ACT.Square, accum_out=stat[:, t:t + 1]).then_inc(ssq, 1)
            act.wait_ge(var, 1)
            nc.scalar.activation(stat[:, 8:12], stat[:, 4:8], ACT.Sqrt).then_inc(std, 1)

            def split_high(r):
                act.wait_ge(w_load[r % 4], 32 * (r // 4 + 1))
                if r >= 2:
                    act.wait_ge(w_used, r - 1)
                n = width(r)
                nc.scalar.activation(r32(w_h[:, r % 2, 0:n]), raw[:, r % 4, 0:n], ACT.Copy).then_inc(w_hi, 1)

            split_high(0)
            split_high(1)
            for i in range(2):
                act.wait_ge(angle, i + 1)
                nc.scalar.activation((sin_t, cos_t)[i], red[i], ACT.Sin).then_inc(table, 1)
            for c in range(NC):
                act.wait_ge(x_tr, c + 1)
                if c == 0:
                    act.wait_ge(pos_cp, 3)
                nc.scalar.activation(r32(h_h[:, c, :]), ps[:, c, :], ACT.Copy, scale=gpre[:, c:c + 1])\
                    .then_inc(h_hi, 1)

            def evacuate(r):
                kind, base, how = tiles[r]
                t = t_of[r]
                act.wait_ge(w_used, r + 1)
                bank = ps[:, t % 2, :]
                if how == ROPE:
                    n = rho_of[r]
                    if n >= 2:
                        act.wait_ge(rotated, n - 1)
                        act.wait_ge(rope_u, n - 1)
                    nc.scalar.activation(xf[:, n % 2, :], bank, ACT.Copy).then_inc(t_evac, 1)
                elif how == COPY:
                    nc.scalar.activation(vc_t, bank, ACT.Copy).then_inc(t_evac, 1)
                else:
                    z = t - 16
                    if z == 0:
                        act.wait_ge(co_mm, 4)
                    nc.scalar.activation(zreg[:, z, :], bank, ACT.Silu).then_inc(t_evac, 1)

            def rope_high(n):
                act.wait_ge(rope_add, n + 1)
                nc.scalar.activation(r32(qk_slot(n)[0]), rr[:, n % 2, :], ACT.Copy).then_inc(rope_hi, 1)

            def values(v, r0):
                act.wait_ge(w_used, r0 + 4)
                bank = ps[:, 4 + v, :]
                if r0 == R_VSG:
                    nc.scalar.activation(v3[:, 0:4, v, 0, :], bank[:, 0:2 * P].rearrange("p (u d) -> p u d", u=4),
                                         ACT.Copy)
                    nc.scalar.activation(gates[:, v, :], bank[:, 2 * P:VSG], ACT.Copy).then_inc(v_hi, 1)
                else:
                    nc.scalar.activation(v3[:, 4:12, v, 0, :], bank.rearrange("p (u d) -> p u d", u=8),
                                         ACT.Copy).then_inc(v_hi, 1)

            for r in range(NPH):
                if r + 2 < NPH + 2:
                    split_high(r + 2)
                if r in t_of:
                    evacuate(r)
                if r - 1 in rho_of and rho_of[r - 1] >= 1:
                    rope_high(rho_of[r - 1])
                if r == 2:
                    act.wait_ge(f_built, 1)
                    nc.scalar.activation(r32(f_h[0]), f_tmp, ACT.Copy).then_inc(f_hid, 1)
                if r == 3:
                    act.wait_ge(f_built, 2)
                    nc.scalar.activation(r32(f_h[1]), f_tmp, ACT.Copy).then_inc(f_hid, 1)
                if r in (R_W1K + 3, R_W1V + 3):
                    i = (r - R_W1K) // 4
                    act.wait_ge(w_used, r + 1)
                    nc.scalar.activation(h1s[i], ps[0:2 * NB, 3 + i, 0:CH], ACT.Silu).then_inc(h1_silu, 1)
                if r == R_W1V - 1 + 2:
                    act.wait_ge(c_mm, 1)
                    act.wait_ge(zeroed, 1)
                    for g in range(2):
                        rows = slice(HD * g, HD * g + HD)
                        last = nc.scalar.activation(r32(kbd_h[rows, CP * g:CP * g + NB]),
                                                    ps[rows, 7, NB * g:NB * g + NB], ACT.Copy)
                    last.then_inc(c_hi, 1)
                if r in (R_VSG + 3, R_VB + 3):
                    for v in range(NT):
                        values(v, r - 3)
                    if r == R_VSG + 3:
                        act.wait_ge(v_hi, 4)
                        nc.scalar.activation(gates[:, :, :], gates[:, :, :], ACT.Exp, scale=-1.0)\
                            .then_inc(gate_e, 1)
                if r == R_VSG + 6:
                    act.wait_ge(cs_dve, 3)
                    nc.scalar.activation(cs, cs, ACT.Exp, scale=SCALE).then_inc(cs_exp, 1)
                if r == R_VSG + 8:
                    for p in range(4):
                        act.wait_ge(cp_tr, p + 1)
                        nc.scalar.activation(pct[0:2 * CP, p, :], ps[0:2 * CP, 4 + p, :], ACT.Copy)\
                            .then_inc(cp_cp, 1)
                if r == R_VSG + 10:
                    for p in range(4):
                        act.wait_ge(co_mm, p + 1)
                        nc.scalar.activation(oc[:, p, :], ps[:, 4 + p, :], ACT.Copy).then_inc(co_cp, 1)

            def exps(U, i):
                qt = 3 - i
                N = P * (qt + 1)
                for a in range(2):
                    act.wait_ge(s_masked, 8 * U + 2 * i + a + 1)
                    pa = prob[:, U % 2, a, off(qt):off(qt) + N]
                    nc.scalar.activation(pa, pa, ACT.Exp, bias=nmx[:, U % 2, qt, a:a + 1], scale=-1.0,
                                         accum_out=den[:, U % 2, qt, a:a + 1]).then_inc(p_exp, 1)

            def pt_high(U, i):
                N = P * (i + 1)
                for a in range(2):
                    m = (2 * i + a) % 4
                    act.wait_ge(pt_ready, 8 * U + 2 * i + a + 1)
                    if 4 * U + i >= 2:
                        act.wait_ge(pv_done, 4 * U + i - 1)
                    nc.scalar.activation(pt_h[:, m, 0:N], ps[:, 2 + m, 0:N], ACT.Copy).then_inc(pt_hi, 1)

            def mix_high(o):
                if o < NSA_PAIRS:
                    act.wait_ge(mix_z, o + 1)
                else:
                    act.wait_ge(o_read, o + NSA_PAIRS + 1)
                nc.scalar.activation(r32(q_h[:, o, :]), mix[:, o % 2, :], ACT.Copy).then_inc(m_hi, 1)

            for i in range(NT):
                exps(0, i)
            for U in range(NU):
                for i in range(NT):
                    if U + 1 < NU:
                        exps(U + 1, i)
                    pt_high(U, i)
                    if i == 1 and U >= 1 and mixed_after(U - 1) is not None:
                        mix_high(mixed_after(U - 1))
            mix_high(PAIRS - 1)
            for r in range(NPH + 2, NW):
                split_high(r)
            for t in range(NT):
                act.wait_ge(y_mm, t + 1)
                for h in range(2):
                    last = nc.scalar.activation(junk[:, S * h:S * h + S], ps[:, 2 * t + h, :], ACT.Square,
                                                accum_out=stat[:, 16 + 2 * t + h:17 + 2 * t + h])
                    last.then_inc(y_sq, 1)
                    act.wait_ge(y_sq, 2 * t + h + 1)
                act.wait_ge(y_var, t + 1)
                nc.scalar.activation(stat[:, 32 + t:33 + t], stat[:, 28 + t:29 + t], ACT.Sqrt).then_inc(y_std, 1)

        @block.vector
        def _(dve):
            V = nc.vector
            dve.wait_ge(p_load, 16)
            dve.wait_ge(c_load, 16)
            k = 0

            def link(ins):
                nonlocal k
                k += 1
                ins.then_inc(chain, 1)
                dve.wait_ge(chain, k)

            link(V.tensor_copy(posf, posi))
            link(V.tensor_scalar(ang, posf, inv, None, ALU.mult))
            link(V.tensor_scalar(trn[0], ang, float(1 / TWO_PI), 0.0, ALU.mult, ALU.add))
            link(V.tensor_scalar(trn[1], ang, float(1 / TWO_PI), 0.25, ALU.mult, ALU.add))
            for i in range(2):
                link(V.tensor_scalar(trn[i], trn[i], ROUND, None, ALU.add))
                link(V.tensor_scalar(trn[i], trn[i], ROUND, None, ALU.subtract))
                link(V.scalar_tensor_tensor(red[i], trn[i], -TP1, ang, ALU.mult, ALU.add))
                link(V.scalar_tensor_tensor(red[i], trn[i], -TP2, red[i], ALU.mult, ALU.add))
                link(V.scalar_tensor_tensor(red[i], trn[i], -TP3, red[i], ALU.mult, ALU.add))
                if i:
                    link(V.tensor_scalar(red[i], red[i], float(np.pi / 2), None, ALU.add))
                V.tensor_scalar(red[i], red[i], PI_IN, -PI_IN, ALU.min, ALU.max).then_inc(angle, 1)
            dve.wait_ge(pos_tr, 1)
            V.tensor_copy(gpre[:, :], ps[:, 7, 0:NC]).then_inc(pos_cp, 1)
            for i in range(2):
                V.tensor_copy(post[i], ps[:, 7, CL * (i + 1):CL * (i + 2)]).then_inc(pos_cp, 1)
            dve.wait_ge(ssq, NT)
            V.tensor_scalar(stat[:, 4:8], stat[:, 0:4], 1.0 / DM, EPS, ALU.mult, ALU.add).then_inc(var, 1)
            dve.wait_ge(std, 1)
            link(V.reciprocal(stat[:, 12:16], stat[:, 8:12]))
            for t in range(NT):
                V.tensor_scalar(x_n[:, t, :], x_in[:, t, :], stat[:, 12 + t:13 + t], None, ALU.mult)\
                    .then_inc(xn_done, 1)

            def split_low(r):
                dve.wait_ge(w_hi, r + 1)
                n = width(r)
                V.tensor_tensor(r32(w_l[:, r % 2, 0:n]), raw[:, r % 4, 0:n], w_h[:, r % 2, 0:n], ALU.subtract)\
                    .then_inc(w_lo, 1)

            split_low(0)
            split_low(1)
            for c in range(NC):
                dve.wait_ge(h_hi, c + 1)
                V.scalar_tensor_tensor(r32(h_l[:, c, :]), ps[:, c, :], gpre[:, c:c + 1], h_h[:, c, :],
                                       ALU.mult, ALU.subtract).then_inc(h_lo, 1)

            def rope(n):
                dve.wait_ge(rotated, n + 1)
                if n:
                    dve.wait_ge(rope_add, n)
                V.tensor_tensor(tt, ps[:, 2, :], sin_t, ALU.mult).then_inc(rope_mul, 1)
                dve.wait_ge(rope_mul, n + 1)
                dve.wait_ge(rope_u, n + 1)
                if n >= 3:
                    dve.wait_ge(rope_hi, n - 2)
                    dve.wait_ge(rope_lo, n - 2)
                dst = rr[:, n % 2, :] if n else kc_t
                V.tensor_tensor(dst, tt, uu[:, n % 2, :], ALU.add).then_inc(rope_add, 1)
                if n:
                    dve.wait_ge(rope_hi, n)
                    hi, lo = qk_slot(n)
                    V.tensor_tensor(r32(lo), rr[:, n % 2, :], hi, ALU.subtract).then_inc(rope_lo, 1)

            def blocks(i):
                src = (kc_t, vc_t)[i]
                fv = f_tmp.rearrange("p (a j g c) -> p a j g c", a=2, j=8, g=2)
                if i:
                    dve.wait_ge(f_lod, 1)
                    dve.wait_ge(t_evac, 2)
                else:
                    dve.wait_ge(rope_add, 1)
                    dve.wait_ge(pos_cp, 3)
                for g in range(2):
                    rows = slice(HD * g, HD * g + HD)
                    sv_ = src[rows, :].rearrange("p (c j t) -> p t j c", j=8, t=2)
                    pv_ = post[i][rows, :].rearrange("p (a j t) -> p a t j", a=2, t=2)
                    for half in range(2):
                        for a in range(2):
                            last = V.tensor_tensor(
                                fv[HD * half:HD * half + HD, a, :, g, :],
                                sv_[:, half, :, a:a + NB],
                                pv_[:, a, half, :].unsqueeze(2).to_broadcast([HD, 8, NB]), ALU.add)
                last.then_inc(f_built, 1)
                dve.wait_ge(f_hid, i + 1)
                V.tensor_tensor(r32(f_l[i]), f_tmp, f_h[i], ALU.subtract).then_inc(f_lod, 1)

            def values_low(v, r0):
                vi = v + (4 if r0 == R_VB else 0)
                n, u0 = (2 * P, 0) if r0 == R_VSG else (S, 4)
                u1 = u0 + n // HD
                rest = vt[:, 0:n].rearrange("p (u d) -> p u d", d=HD)
                dve.wait_ge(v_hi, vi + 1)
                if vi:
                    dve.wait_ge(v_done, vi)
                V.tensor_tensor(rest, ps[:, 4 + v, 0:n].rearrange("p (u d) -> p u d", d=HD),
                                v3[:, u0:u1, v, 0, :], ALU.subtract).then_inc(v_rest, 1)
                dve.wait_ge(v_rest, vi + 1)
                V.tensor_copy(v3[:, u0:u1, v, 1, :], rest).then_inc(v_mid, 1)
                dve.wait_ge(v_mid, vi + 1)
                V.tensor_tensor(v3[:, u0:u1, v, 2, :], rest, v3[:, u0:u1, v, 1, :], ALU.subtract)\
                    .then_inc(v_done, 1)

            vt = tt
            for r in range(NPH):
                split_low(r + 2)
                if r - 1 in rho_of:
                    rope(rho_of[r - 1])
                if r in (2, 3):
                    blocks(r - 2)
                if r == R_W1V:
                    dve.wait_ge(h1_tr, 1)
                    V.tensor_copy(h1kt, ps[:, 5, 0:4 * NB].rearrange("p (j n) -> p j n", j=2)).then_inc(h1_cp, 1)
                if r == R_W1V + 1:
                    dve.wait_ge(c_hi, 1)
                    for g in range(2):
                        rows = slice(HD * g, HD * g + HD)
                        last = V.tensor_tensor(r32(kbd_l[rows, CP * g:CP * g + NB]),
                                               ps[rows, 7, NB * g:NB * g + NB],
                                               kbd_h[rows, CP * g:CP * g + NB], ALU.subtract)
                    last.then_inc(c_lo, 1)
                if r == R_W1V + 4:
                    dve.wait_ge(h1_tr, 2)
                    dve.wait_ge(zeroed, 1)
                    for j in range(2):
                        last = V.tensor_copy(h1vt[:, j, :, 0:NB],
                                             ps[:, 6, 2 * NB * j:2 * NB * (j + 1)]
                                             .rearrange("p (g n) -> p g n", g=2))
                    last.then_inc(h1_cp, 1)
                if r == R_W1V + 5:
                    dve.wait_ge(c_mm, 2)
                    for g in range(2):
                        rows = slice(CP * g, CP * g + CP)
                        last = V.tensor_copy(vbd[rows, HD * g:HD * g + HD], ps[rows, 3, 0:HD])
                    last.then_inc(c_lo, 1)
                if r in (R_VSG + 3, R_VB + 3):
                    for v in range(NT):
                        values_low(v, r - 3)
                    if r == R_VSG + 3:
                        dve.wait_ge(gate_e, 1)
                        link(V.tensor_scalar(gates[:, :, :], gates[:, :, :], 1.0, None, ALU.add))
                        link(V.reciprocal(gates[:, :, :], gates[:, :, :]))
                        gv = gates[:, :, :].rearrange("p t (b a q) -> p b a q t", b=3, a=2)
                        for b in range(2):
                            for a in range(2):
                                last = V.tensor_copy(gw[:, b:2 * NSA_PAIRS:2, :, a], gv[:, b + 1, a, :, :])
                        last.then_inc(gate_s, 1)
                if r == R_VSG + 5:
                    dve.wait_ge(cs_mm, 1)
                    dve.wait_ge(t_load, 16)
                    for b in range(2):
                        sc = ps[:, 4 + b, :].rearrange("p (t h c) -> p t h c", t=2, h=8)
                        last = V.tensor_tensor(cs[:, 2 * b:2 * b + 2, :, :], sc,
                                               cadd[:, 2 * b:2 * b + 2, :].unsqueeze(2).to_broadcast([P, 2, 8, CP]),
                                               ALU.add)
                    last.then_inc(cs_dve, 1)
                    dve.wait_ge(cs_dve, 1)
                    csf = cs.rearrange("p t h c -> p (t h) c")
                    V.tensor_reduce(cden[:, 0, :], csf, AX, ALU.max).then_inc(cs_dve, 1)
                    dve.wait_ge(cs_dve, 2)
                    V.tensor_tensor(csf, csf, cden[:, 0, :].unsqueeze(2).to_broadcast([P, NT * 8, CP]),
                                    ALU.subtract).then_inc(cs_dve, 1)
                if r == R_VSG + 6:
                    dve.wait_ge(cs_exp, 1)
                    csf = cs.rearrange("p t h c -> p (t h) c")
                    link(V.tensor_tensor(cs, cs, cval.unsqueeze(2).to_broadcast([P, NT, 8, CP]), ALU.mult))
                    link(V.tensor_reduce(cden[:, 0, :], csf, AX, ALU.add))
                    link(V.tensor_scalar(cden[:, 1, :], cden[:, 0, :], 1e-30, None, ALU.max))
                    link(V.reciprocal(cden[:, 2, :], cden[:, 1, :]))
                    link(V.tensor_tensor(cden[:, 1, :].rearrange("p (t q a) -> p t q a", t=NT, a=2),
                                         cden[:, 2, :].rearrange("p (t q a) -> p t q a", t=NT, a=2),
                                         gates[:, :, 0:8].rearrange("p t (a q) -> p t q a", a=2), ALU.mult))
                    V.tensor_tensor(csf, csf, cden[:, 1, :].unsqueeze(2).to_broadcast([P, NT * 8, CP]),
                                    ALU.mult).then_inc(cs_dve, 1)

            def mask(U, i):
                qt = 3 - i
                N = P * (qt + 1)
                bias = causal if U < 2 * NSA_PAIRS else dilated
                dve.wait_ge(s_ready, 4 * U + i + 1)
                if i == 0 and U >= 2:
                    dve.wait_ge(pt_ready, 8 * (U - 1))
                for a in range(2):
                    V.tensor_tensor_reduce(out=prob[:, U % 2, a, off(qt):off(qt) + N], in0=ps[:, a, 0:N],
                                           in1=bias[:, S - N:S], scale=-SCALE, scalar=BIG, op0=ALU.add,
                                           op1=ALU.min, accum_out=nmx[:, U % 2, qt, a:a + 1]).then_inc(s_masked, 1)

            def weigh(U, i):
                qt = 3 - i
                n = 4 * U + i
                dve.wait_ge(p_exp, 2 * n + 2)
                if i == 0 and U >= 2:
                    dve.wait_ge(pn_g, 2 * (U - 1))
                V.reciprocal(rw[:, U % 2, qt, :], den[:, U % 2, qt, :]).then_inc(p_rec, 1)
                dve.wait_ge(p_rec, n + 1)
                V.tensor_tensor(rw[:, U % 2, qt, :], rw[:, U % 2, qt, :], gw[:, U, qt, :], ALU.mult)\
                    .then_inc(w_ready, 1)
                if qt < 2:
                    dve.wait_ge(w_ready, n + 1)
                    N = P * (qt + 1)
                    for a in range(2):
                        pa = prob[:, U % 2, a, off(qt):off(qt) + N]
                        last = V.tensor_scalar(pa, pa, rw[:, U % 2, qt, a:a + 1], None, ALU.mult)
                    last.then_inc(pn_v, 1)

            def pt_low(U, i):
                N = P * (i + 1)
                for a in range(2):
                    m = (2 * i + a) % 4
                    dve.wait_ge(pt_hi, 8 * U + 2 * i + a + 1)
                    V.tensor_tensor(pt_l[:, m, 0:N], ps[:, 2 + m, 0:N], pt_h[:, m, 0:N], ALU.subtract)\
                        .then_inc(pt_lo, 1)

            def collect(U):
                dve.wait_ge(pv_done, 4 * U + 4)
                bank = ps[:, 6 + U % 2, :]
                if U < 2 * NSA_PAIRS:
                    p = U // 2
                    mx = mix[:, p % 2, :]
                    if U % 2 == 0:
                        if p >= 2:
                            dve.wait_ge(m_hi, p - 1)
                            dve.wait_ge(m_lo, p - 1)
                        if p == 0:
                            dve.wait_ge(co_cp, 4)
                        V.tensor_tensor(mx, bank, oc[:, p, :], ALU.add).then_inc(o_read, 1)
                    else:
                        dve.wait_ge(o_read, U)
                        V.tensor_tensor(mx, bank, mx, ALU.add).then_inc(o_read, 1)
                        dve.wait_ge(o_read, U + 1)
                        V.tensor_tensor(mx, mx, zreg[:, p, :], ALU.mult).then_inc(mix_z, 1)
                else:
                    o = U - NSA_PAIRS
                    dve.wait_ge(m_hi, o - 1)
                    dve.wait_ge(m_lo, o - 1)
                    V.tensor_tensor(mix[:, o % 2, :], bank, zreg[:, o, :], ALU.mult).then_inc(o_read, 1)

            def mix_low(o):
                dve.wait_ge(m_hi, o + 1)
                V.tensor_tensor(r32(q_l[:, o, :]), mix[:, o % 2, :], q_h[:, o, :], ALU.subtract).then_inc(m_lo, 1)

            dve.wait_ge(w_used, NPH)
            dve.wait_ge(zeroed, 2)
            dve.wait_ge(gate_s, 1)
            for i in range(NT):
                mask(0, i)
                weigh(0, i)
            for U in range(NU):
                for i in range(NT):
                    if U + 1 < NU:
                        mask(U + 1, i)
                    pt_low(U, i)
                    if i == 0 and U >= 1:
                        collect(U - 1)
                    if i == 2 and U >= 1 and mixed_after(U - 1) is not None:
                        mix_low(mixed_after(U - 1))
                    if U + 1 < NU:
                        weigh(U + 1, i)
            collect(NU - 1)
            mix_low(PAIRS - 1)
            for r in range(NPH + 2, NW):
                split_low(r)
            dve.wait_ge(g_load, 16)
            dve.wait_ge(r_load, 16 * NT)
            for t in range(NT):
                dve.wait_ge(y_sq, 2 * t + 2)
                link(V.tensor_tensor(stat[:, 24 + t:25 + t], stat[:, 16 + 2 * t:17 + 2 * t],
                                     stat[:, 17 + 2 * t:18 + 2 * t], ALU.add))
                V.tensor_scalar(stat[:, 28 + t:29 + t], stat[:, 24 + t:25 + t], 1.0 / DM, EPS, ALU.mult, ALU.add)\
                    .then_inc(y_var, 1)
                dve.wait_ge(y_std, t + 1)
                link(V.reciprocal(stat[:, 36 + t:37 + t], stat[:, 32 + t:33 + t]))
                for h in range(2):
                    last = V.scalar_tensor_tensor(y_out[:, t, S * h:S * h + S], ps[:, 2 * t + h, :],
                                                  stat[:, 36 + t:37 + t], gpost[:, S * h:S * h + S],
                                                  ALU.mult, ALU.mult)
                last.then_inc(y_mul, 1)
                dve.wait_ge(y_mul, t + 1)
                V.tensor_tensor(y_out[:, t, :], y_out[:, t, :], x_in[:, t, :], ALU.add).then_inc(y_add, 1)

        @block.tensor
        def _(pe):
            T = nc.tensor
            pe.wait_ge(c_load, 16)
            pe.wait_ge(k_load, 16 * 8)
            T.transpose(ps[:, 7, 0:NC], grow, ident[0:NC, 0:NC])
            for i in range(2):
                last = T.transpose(ps[:, 7, CL * (i + 1):CL * (i + 2)], posr[i], ident[0:CL, 0:CL])
            last.then_inc(pos_tr, 1)
            pe.wait_ge(xn_done, NT)
            for c in range(NC):
                if c == NC - 1:
                    pe.wait_ge(pos_cp, 3)
                for t in range(NT):
                    last = T.transpose(ps[:, c, P * t:P * t + P], x_n[:, t, P * c:P * c + P], ident)
                last.then_inc(x_tr, 1)
            pe.wait_ge(h_lo, NC)

            def three(dst, lh, ll, rh, rl, first, last):
                T.matmul(dst, r32(lh), r32(rh), start=first, stop=False)
                T.matmul(dst, r32(ll), r32(rh), start=False, stop=False)
                return T.matmul(dst, r32(lh), r32(rl), start=False, stop=last)

            def main(r):
                kind, j, how = tiles[r]
                pe.wait_ge(w_lo, r + 1)
                wh, wl = w_h[:, r % 2, :], w_l[:, r % 2, :]
                if kind in ("proj", "pair"):
                    t = t_of[r]
                    if t >= 2:
                        pe.wait_ge(t_evac, t - 1)
                    for c in range(NC):
                        cc = slice(P * c, P * c + P)
                        last = three(ps[:, t % 2, :], wh[:, cc], wl[:, cc], h_h[:, c, :], h_l[:, c, :],
                                     c == 0, c == NC - 1)
                elif kind in ("w1k", "w1v"):
                    i = 0 if kind == "w1k" else 1
                    if j == 0:
                        pe.wait_ge(f_lod, i + 1)
                    for jj in range(4):
                        st = 4 * j + jj
                        fc = slice(2 * NB * st, 2 * NB * (st + 1))
                        wc = slice(CH * jj, CH * jj + CH)
                        last = three(ps[0:2 * NB, 3 + i, 0:CH], f_h[i][:, fc], f_l[i][:, fc], wh[:, wc], wl[:, wc],
                                     st == 0, st == 15)
                elif kind in ("vsg", "vb"):
                    N = VSG if kind == "vsg" else S
                    if kind == "vsg" and j == 0:
                        pe.wait_ge(c_lo, 2)
                    if kind == "vb" and j == 0:
                        pe.wait_ge(co_cp, 4)
                    for t in range(NT):
                        tc = slice(P * t, P * t + P)
                        for jj in range(2):
                            c = 2 * j + jj
                            wc = slice(N * jj, N * jj + N)
                            last = three(ps[:, 4 + t, 0:N], h_h[:, c, tc], h_l[:, c, tc], wh[:, wc], wl[:, wc],
                                         c == 0, c == NC - 1)
                last.then_inc(w_used, 1)

            def rotate(n):
                pe.wait_ge(t_evac, t_of[ropes[n]] + 1)
                if n:
                    pe.wait_ge(rope_mul, n)
                T.matmul(ps[:, 2, :], rot, xf[:, n % 2, :], start=True, stop=True).then_inc(rotated, 1)

            for r in range(NPH):
                main(r)
                if r - 1 in rho_of:
                    rotate(rho_of[r - 1])
                if r in (R_W1V, R_W1V + 4):
                    i = (r - R_W1V) // 4
                    pe.wait_ge(h1_silu, i + 1)
                    for j in range(2):
                        last = T.transpose(ps[:, 5 + i, 2 * NB * j:2 * NB * (j + 1)], h1s[i][:, P * j:P * j + P],
                                           ident[0:2 * NB, 0:2 * NB])
                    last.then_inc(h1_tr, 1)
                if r == R_W1V + 1:
                    pe.wait_ge(h1_cp, 1)
                    for j in range(2):
                        last = T.matmul(ps[:, 7, 0:2 * NB], w2k[:, j, :], h1kt[:, j, :], start=j == 0, stop=j == 1)
                    last.then_inc(c_mm, 1)
                if r == R_W1V + 5:
                    pe.wait_ge(h1_cp, 2)
                    for j in range(2):
                        last = T.matmul(ps[0:2 * CP, 3, 0:HD], h1vt[:, j, :, :].rearrange("p g n -> p (g n)"),
                                        w2v[:, j, :], start=j == 0, stop=j == 1)
                    last.then_inc(c_mm, 1)
                if r == R_VSG + 4:
                    pe.wait_ge(v_done, 4)
                    pe.wait_ge(c_lo, 1)
                    pe.wait_ge(rope_lo, 6)
                    for t in range(NT):
                        for p in range(4):
                            tc = slice(P * t, P * t + P)
                            o = 256 * (t % 2) + 64 * p
                            last = three(ps[:, 4 + t // 2, o:o + 64], q_h[:, p, tc], q_l[:, p, tc],
                                         kbd_h[:, :], kbd_l[:, :], True, True)
                    last.then_inc(cs_mm, 1)
                if r == R_VSG + 8:
                    pe.wait_ge(cs_dve, 4)
                    for p in range(4):
                        for t in range(NT):
                            last = T.transpose(ps[0:2 * CP, 4 + p, P * t:P * t + P],
                                               cs[:, t, 2 * p:2 * p + 2, :].rearrange("p h c -> p (h c)"), ident)
                        last.then_inc(cp_tr, 1)
                if r == R_VSG + 10:
                    for p in range(4):
                        pe.wait_ge(cp_cp, p + 1)
                        T.matmul(ps[:, 4 + p, :], vbd, pct[0:2 * CP, p, :], start=True, stop=True)\
                            .then_inc(co_mm, 1)

            def scores(U, i):
                qt = 3 - i
                N = max(P * (qt + 1), 2 * P)
                p, kk, _ = unit(U)
                if 4 * U + i >= 1:
                    pe.wait_ge(s_masked, 8 * U + 2 * i)
                for ql, kr in ((q_h, k_h), (q_l, k_h), (q_h, k_l)):
                    for a in range(2):
                        rows = slice(HD * a, HD * a + HD)
                        last = T.matmul(ps[:, a, 0:N], r32(ql[rows, p, P * qt:P * qt + P]), r32(kr[rows, kk, 0:N]),
                                        start=ql is q_h and kr is k_h, stop=kr is k_l)
                last.then_inc(s_ready, 1)

            def transposes(U, i):
                kt = 3 - i
                if kt >= 2:
                    pe.wait_ge(pn_g, 2 * U + i + 1)
                else:
                    pe.wait_ge(pn_v, 2 * U + i - 1)
                for a in range(2):
                    n = 8 * U + 2 * i + a
                    m = (2 * i + a) % 4
                    if n >= 4:
                        pe.wait_ge(pt_lo, n - 3)
                    for qt in range(kt, NT):
                        src = prob[:, U % 2, a, off(qt) + P * kt:off(qt) + P * kt + P]
                        last = T.transpose(ps[:, 2 + m, P * (qt - kt):P * (qt - kt) + P], src, ident)
                    last.then_inc(pt_ready, 1)

            def outputs(U, i):
                kt = 3 - i
                vu = unit(U)[2]
                pe.wait_ge(pt_lo, 8 * U + 2 * i + 2)
                if i == 0 and U >= 2:
                    pe.wait_ge(o_read, U - 1)
                N = P * (i + 1)
                for part, pt in ((0, pt_h), (1, pt_h), (2, pt_h), (0, pt_l), (1, pt_l)):
                    for a in range(2):
                        m = (2 * i + a) % 4
                        dst = ps[HD * a:HD * a + HD, 6 + U % 2, P * kt:S]
                        first = part == 0 and pt is pt_h
                        for c in ((slice(0, P), slice(P, N)) if first and i else (slice(0, N),)):
                            last = T.matmul(dst[:, c], v3[:, vu + a, kt, part, :], pt[:, m, c],
                                            start=first and i == 0, stop=i == 3 and part == 1 and pt is pt_l)
                last.then_inc(pv_done, 1)

            pe.wait_ge(rope_lo, len(ropes) - 1)
            pe.wait_ge(t_evac, len(proj))
            pe.wait_ge(v_done, 2 * NT)
            for i in range(NT):
                scores(0, i)
            for U in range(NU):
                for i in range(NT):
                    if U + 1 < NU:
                        scores(U + 1, i)
                    transposes(U, i)
                    if i:
                        outputs(U, i - 1)
                    elif U:
                        outputs(U - 1, NT - 1)
            outputs(NU - 1, NT - 1)

            pe.wait_ge(o_read, NU)
            for o in range(PAIRS):
                r = NPH + o
                pe.wait_ge(w_lo, r + 1)
                pe.wait_ge(m_lo, o + 1)
                for t in range(NT):
                    tc = slice(P * t, P * t + P)
                    for h in range(2):
                        hc = slice(S * h, S * h + S)
                        last = three(ps[:, 2 * t + h, :], q_h[:, o, tc], q_l[:, o, tc], w_h[:, r % 2, hc],
                                     w_l[:, r % 2, hc], o == 0, o == PAIRS - 1)
                    if o == PAIRS - 1:
                        last.then_inc(y_mm, 1)
                if o < PAIRS - 1:
                    last.then_inc(w_used, 1)


def constants():
    c = np.zeros((P, C_END), np.float32)
    c[:, C_ID:C_ID + P] = np.eye(P)
    half = HD // 8
    for base in (0, HD):
        for i in range(half):
            c[base + half + i, C_ROT + base + i] = -1.0
            c[base + i, C_ROT + base + half + i] = 1.0
    inv = np.float32(1.0) / (np.float32(500000.0) ** (np.arange(0, 2 * half, 2, dtype=np.float32) / np.float32(2 * half)))
    for base in (0, half, HD, HD + half):
        c[base:base + half, C_INV] = inv
    i = np.arange(P)[:, None]
    dist = i + 3 * P - np.arange(S)[None, :]
    c[:, C_CAUSAL:C_CAUSAL + S] = np.where(dist >= 0, 0.0, NEG)
    count = ((dist <= 128).astype(int) + (dist % 4 == 0) + (dist % 16 == 0)) * (dist >= 0)
    c[:, C_DIL:C_DIL + S] = np.where(count > 0, np.log(np.maximum(count, 1)) / SCALE, NEG)
    tok = np.arange(P)[:, None, None] + P * np.arange(NT)[None, :, None]
    blk = np.arange(CP)[None, None, :]
    ok = (blk < NB) & (CS * blk + CL - 1 <= tok)
    c[:, C_CADD:C_CVAL] = np.where(ok, 0.0, NEG).reshape(P, -1)
    c[:, C_CVAL:C_END] = ok.reshape(P, -1)
    return c


def kernel(**inputs):
    import concourse.bacc as _bacc
    from concourse.bass_utils import run_bass_kernel_spmd as _run

    nc = _bacc.Bacc("TRN2", target_bir_lowering=False, num_devices=1)
    arrays, args = {}, []
    names = ["x", "positions", "pre_norm_g", "w_in", "cmp_k_pos", "cmp_k_w1", "cmp_k_w2", "cmp_v_pos", "cmp_v_w1",
             "cmp_v_w2", "w_out", "post_norm_g"]
    for name in names:
        a = np.ascontiguousarray(inputs[name])
        if name not in ("x", "positions"):
            a = a[0]
        arrays[f"in_{name}"] = np.ascontiguousarray(a)
    arrays["in_consts"] = constants()
    for name, a in arrays.items():
        args.append(nc.dram_tensor(name, a.shape, mybir.dt.from_np(a.dtype), kind="ExternalInput").ap())
    args.append(nc.dram_tensor("out_0", (1, S, DM), F32, kind="ExternalOutput").ap())
    hymba_kernel(nc, *args)
    r = _run(nc, [arrays], core_ids=[0])
    return r.results[0]["out_0"]
```

```python
from contextlib import ExitStack

import numpy as np

import concourse.bass as bass
from concourse import mybir

ALU = mybir.AluOpType
ACT = mybir.ActivationFunctionType
AX = mybir.AxisListType.X
F32 = mybir.dt.float32
F32R = mybir.dt.float32r
F16 = mybir.dt.float16
BF16 = mybir.dt.bfloat16
I32 = mybir.dt.int32

P = 128
S = 512
DM = 1024
HD = 64
NT = S // P
NC = DM // P
NSA_PAIRS = 4
DIL_PAIRS = 4
PAIRS = NSA_PAIRS + DIL_PAIRS
CL, CS, CH = 32, 16, 256
NB = (S - CL) // CS + 1
CP = 32
EPS = 1e-6
SCALE = HD ** -0.5
NEG = -1e30
BIG = 3e38

COL = dict(q_a=0, k_cmp=512, v_cmp=640, k_slc=768, v_slc=896, k_win=1024, v_win=1152, gate=1280,
           z_a=1304, q_b=1816, k_b=2328, v_b=2840, z_b=3352)
NG = 24
VSG = 2 * P + NG

C_ID, C_ROT, C_INV = 0, P, 2 * P
C_CAUSAL = 2 * P + 1
C_DIL = C_CAUSAL + S
C_CADD = C_DIL + S
C_CVAL = C_CADD + NT * CP
C_END = C_CVAL + NT * CP

TWO_PI = 2 * np.pi
TP1 = 6.28125
TP2 = float(np.round((TWO_PI - TP1) * 2 ** 20) / 2 ** 20)
TP3 = float(np.float32(TWO_PI - TP1 - TP2))
ROUND = 1.5 * 2 ** 23
PI_IN = 3.1415925

ROPE, COPY, SILU = "rope", "copy", "silu"


def weight_tiles():
    tiles = [("proj", COL[name], how)
             for name, how in (("k_cmp", ROPE), ("v_cmp", COPY), ("k_slc", ROPE), ("k_win", ROPE))]
    for j in range(4):
        tiles += [("pair", COL["q_a"] + HD * j, ROPE), ("w1k", j, None)]
    tiles += [("vsg", j, None) for j in range(4)]
    for j in range(4):
        tiles += [("w1v", j, None), ("proj", COL["q_b"] + P * j, ROPE)]
    tiles += [("proj", COL["k_b"] + P * j, ROPE) for j in range(4)]
    tiles += [("vb", j, None) for j in range(4)]
    tiles += [("pair", COL["z_a"] + HD * j, SILU) for j in range(4)]
    tiles += [("proj", COL["z_b"] + P * j, SILU) for j in range(4)]
    tiles += [("out", j, None) for j in range(8)]
    return tiles


def hymba_kernel(nc, x, positions, pre_g, w_in, ck_pos, ck_w1, ck_w2, cv_pos, cv_w1, cv_w2, w_out, post_g,
                 consts, out):
    tiles = weight_tiles()
    NW = len(tiles)
    NPH = NW - 8
    proj = [r for r in range(NW) if tiles[r][0] in ("proj", "pair")]
    t_of = {r: t for t, r in enumerate(proj)}
    ropes = [r for r in proj if tiles[r][2] == ROPE]
    rho_of = {r: n for n, r in enumerate(ropes)}
    R_VSG, R_VB, R_W1K, R_W1V = (tiles.index((kind, 0, None)) for kind in ("vsg", "vb", "w1k", "w1v"))
    R_QB = tiles.index(("proj", COL["q_b"], ROPE))
    R_KB = tiles.index(("proj", COL["k_b"], ROPE))
    G = 4 * (2 * NSA_PAIRS + DIL_PAIRS)

    ctx = ExitStack()
    with ctx:
        def sb(name, shape, dt=F32):
            return ctx.enter_context(nc.sbuf_tensor(name, shape, dt))

        def sem(name):
            return ctx.enter_context(nc.semaphore(name))

        def r32(ap):
            return ap.bitcast(F32R)

        cst = sb("cst", [P, C_END])
        ident = cst[:, C_ID:C_ID + P]
        rot = cst[:, C_ROT:C_ROT + P]
        inv = cst[:, C_INV:C_INV + 1]
        causal = cst[:, C_CAUSAL:C_CAUSAL + S]
        dilated = cst[:, C_DIL:C_DIL + S]
        cadd = cst[:, C_CADD:C_CADD + NT * CP].rearrange("p (t c) -> p t c", t=NT)
        cval = cst[:, C_CVAL:C_CVAL + NT * CP].rearrange("p (t c) -> p t c", t=NT)
        raw = sb("raw", [P, 4, DM])
        w_h = sb("w_h", [P, 2, DM])
        w_l = sb("w_l", [P, 2, DM])
        q_l = sb("q_l", [P, PAIRS, S])
        k_h = sb("k_h", [P, 2 + DIL_PAIRS, S])
        k_l = sb("k_l", [P, 2 + DIL_PAIRS, S])
        zreg = sb("zreg", [P, PAIRS, S])
        vreg = sb("vreg", [P, 12 * 4 * 3 * HD // 2])
        v3 = vreg[:, :].bitcast(BF16).rearrange("p (u k s d) -> p u k s d", u=12, k=NT, s=3)
        x_in = vreg[:, 0:NT * DM].rearrange("p (t n) -> p t n", t=NT)
        gpre = sb("gpre", [P, NC])
        stat = sb("stat", [P, 64])
        gates = sb("gates", [P, NT, NG])
        gw = sb("gw", [P, 12, NT, 2])
        den = sb("den", [P, 2, NT, 2])
        nmx = sb("nmx", [P, 2, NT, 2])
        rw = sb("rw", [P, 2, NT, 2])
        cden = sb("cden", [P, 3, NT * 8])

        def overlay(*specs):
            with ExitStack() as own:
                return [own.enter_context(nc.sbuf_tensor(n, [P, w], F32))[:, :] for n, w in specs]

        x_n, = overlay(("x_n", NT * DM))
        x_n = x_n.rearrange("p (t n) -> p t n", t=NT)
        q_h = sb("q_h", [P, PAIRS, S])

        h_h, h_l = (t.rearrange("p (c s) -> p c s", c=NC) for t in overlay(("h_h", NC * S), ("h_l", NC * S)))
        PW = 1280
        prob, pt_h, pt_l = overlay(("prob", 4 * PW), ("pt_h", PW), ("pt_l", PW))
        prob = prob.rearrange("p (u a n) -> p u a n", u=2, a=2)
        pt_h = pt_h.bitcast(F16).rearrange("p (a n) -> p a n", a=2)
        pt_l = pt_l.bitcast(F16).rearrange("p (a n) -> p a n", a=2)
        y_out, junk = overlay(("y_out", NT * DM), ("junk", DM))
        y_out = y_out.rearrange("p (t n) -> p t n", t=NT)
        sb("first_area", [P, 2 * NC * S])

        FW = 16 * 2 * NB
        fkh, fkl, fvh, fvl, _, f_tmp, kc_t, vc_t, xf, uu, tt, rr, cos_t, sin_t = overlay(
            ("fkh", FW), ("fkl", FW), ("fvh", FW), ("fvl", FW), ("gap", 4 * (1024 - FW)), ("f_tmp", 1024),
            ("kc_t", S), ("vc_t", S), ("xf", 2 * S), ("uu", 2 * S), ("tt", S), ("rr", 2 * S),
            ("cos_t", S), ("sin_t", S))
        f_h, f_l = (fkh, fvh), (fkl, fvl)
        f_tmp = f_tmp[:, 0:FW]
        xf, uu, rr = (t.rearrange("p (b s) -> p b s", b=2) for t in (xf, uu, rr))
        oc, pct, cs = overlay(("oc", 4 * S), ("pct", 4 * S), ("cs", NT * 8 * CP))
        oc = oc.rearrange("p (a s) -> p a s", a=4)
        pct = pct.rearrange("p (a s) -> p a s", a=4)
        cs = cs.rearrange("p (t h c) -> p t h c", t=NT, h=8)
        _, gpost, mix = overlay(("gap2", 8 * S), ("gpost", DM), ("mix", 2 * S))
        mix = mix.rearrange("p (m n) -> p m n", m=2)
        startup, = overlay(("startup", 10752))
        sb("second_area", [P, 10752])
        posi = startup[:, 0:512].bitcast(I32)
        posf = startup[:, 512:1024]
        ang = startup[:, 1024:1536]
        trn = [startup[:, 1536:2048], startup[:, 2048:2560]]
        red = [startup[:, 2560:3072], startup[:, 3072:3584]]
        xjunk = startup[:, 5632:5632 + DM]
        zf = zreg[:, :, :].rearrange("p a s -> p (a s)")
        w2k = zf[:, 0:256].rearrange("p (j n) -> p j n", j=2)
        w2v = zf[:, 256:384].rearrange("p (j n) -> p j n", j=2)
        posr = [zf[0:CL, 384 + 128 * i:512 + 128 * i] for i in range(2)]
        grow = zf[0:NC, 2112:2240]
        post = [zf[:, 640 + 32 * i:672 + 32 * i] for i in range(2)]
        h1s = [zf[0:2 * NB, 704 + 256 * i:960 + 256 * i] for i in range(2)]
        h1kt = zf[:, 1216:1216 + 4 * NB].rearrange("p (j n) -> p j n", j=2)
        h1vt = zf[:, 1344:1472].rearrange("p (j g n) -> p j g n", j=2, g=2)
        kbd_h = sb("kbd_h", [P, 2 * CP])
        kbd_l = sb("kbd_l", [P, 2 * CP])
        vbd = zf[0:2 * CP, 1856:1856 + P]

        ps = ctx.enter_context(nc.psum_tensor("ps", [P, 8, S], F32))

        x_load = [sem(f"x_load{t}") for t in range(NT)]
        c_load = sem("c_load")
        t_load = sem("t_load")
        p_load = sem("p_load")
        g_load = sem("g_load")
        k_load = sem("k_load")
        w_load = [sem(f"w_load{s}") for s in range(4)]
        w_hi, w_lo, w_used = sem("w_hi"), sem("w_lo"), sem("w_used")
        ssq, var, std, rstd, xn_done = sem("ssq"), sem("var"), sem("std"), sem("rstd"), sem("xn_done")
        angle, table = sem("angle"), sem("table")
        x_tr, h_hi, h_lo = sem("x_tr"), sem("h_hi"), sem("h_lo")
        t_evac, rotated = sem("t_evac"), sem("rotated")
        rope_mul, rope_u, rope_add, rope_hi, rope_lo = (sem("rope_mul"), sem("rope_u"), sem("rope_add"),
                                                        sem("rope_hi"), sem("rope_lo"))
        zeroed = sem("zeroed")
        pos_tr, pos_cp = sem("pos_tr"), sem("pos_cp")
        f_built, f_hid, f_lod = sem("f_built"), sem("f_hid"), sem("f_lod")
        h1_silu, h1_tr, h1_cp, c_mm, c_hi, c_lo = (sem("h1_silu"), sem("h1_tr"), sem("h1_cp"), sem("c_mm"),
                                                   sem("c_hi"), sem("c_lo"))
        v_hi, v_rest, v_mid, v_done = sem("v_hi"), sem("v_rest"), sem("v_mid"), sem("v_done")
        gate_e, gate_s = sem("gate_e"), sem("gate_s")
        cs_mm, cs_dve, cs_exp, cp_tr, cp_cp, co_mm, co_cp = (sem("cs_mm"), sem("cs_dve"), sem("cs_exp"),
                                                            sem("cp_tr"), sem("cp_cp"), sem("co_mm"),
                                                            sem("co_cp"))
        s_ready, s_masked, p_exp, w_ready = sem("s_ready"), sem("s_masked"), sem("p_exp"), sem("w_ready")
        p_rec, pn_v, pn_g = sem("p_rec"), sem("pn_v"), sem("pn_g")
        pt_ready, pt_hi, pt_lo, pv_done = sem("pt_ready"), sem("pt_hi"), sem("pt_lo"), sem("pv_done")
        o_read, mix_add, mix_z, m_hi, m_lo = (sem("o_read"), sem("mix_add"), sem("mix_z"), sem("m_hi"),
                                              sem("m_lo"))
        y_mm, y_sq, y_var, y_std, y_rstd, y_mul, y_add, y_out_s = (
            sem("y_mm"), sem("y_sq"), sem("y_var"), sem("y_std"), sem("y_rstd"), sem("y_mul"), sem("y_add"),
            sem("y_out"))
        r_load = sem("r_load")
        chain = sem("chain")

        w_in_v = w_in.rearrange("(c p) n -> p c n", p=P)
        w1_v = {"w1k": ck_w1.rearrange("(j p) n -> p j n", p=P), "w1v": cv_w1.rearrange("(j p) n -> p j n", p=P)}
        x_v = x.rearrange("b (t p) n -> p (b t) n", p=P)
        out_v = out.rearrange("b (t p) n -> p (b t) n", p=P)

        def off(qt):
            return P * qt * (qt + 1) // 2

        def width(r):
            return 2 * VSG if tiles[r][0] == "vsg" else DM

        def unit(U):
            if U < 2 * NSA_PAIRS:
                return U // 2, U % 2, 2 * (U % 2)
            i = U - 2 * NSA_PAIRS
            return NSA_PAIRS + i, 2 + i, 4 + 2 * i

        def qk_slot(n):
            if n < 3:
                return k_h[:, n - 1, :], k_l[:, n - 1, :]
            if n < 11:
                return q_h[:, n - 3, :], q_l[:, n - 3, :]
            return k_h[:, n - 9, :], k_l[:, n - 9, :]

        def mixed_after(U):
            if U < 2 * NSA_PAIRS:
                return U // 2 if U % 2 else None
            return U - NSA_PAIRS

        NU = 2 * NSA_PAIRS + DIL_PAIRS

        block = ctx.enter_context(nc.Block())

        @block.sync
        def _(sp):
            for t in range(NT):
                sp.dma_start(x_in[:, t, :], x_v[:, t, :]).then_inc(x_load[t], 16)

            def load_weights(r):
                kind, j, _ = tiles[r]
                done = w_load[r % 4]
                if r >= 4:
                    sp.wait_ge(w_lo, r - 3)
                if kind == "proj":
                    v = raw[:, r % 4, :].rearrange("p (c n) -> p c n", c=NC)
                    for h in range(2):
                        sp.dma_start(v[:, 4 * h:4 * h + 4, :], w_in_v[:, 4 * h:4 * h + 4, j:j + P]).then_inc(done, 16)
                elif kind == "pair":
                    v = raw[:, r % 4, :].rearrange("p (c n) -> p c n", c=NC)
                    for h in range(2):
                        sp.dma_start(v[:, :, HD * h:HD * h + HD],
                                     w_in_v[:, :, j + 4 * HD * h:j + 4 * HD * h + HD]).then_inc(done, 16)
                elif kind in w1_v:
                    v = raw[:, r % 4, :].rearrange("p (c n) -> p c n", c=4)
                    for h in range(2):
                        sp.dma_start(v[:, 2 * h:2 * h + 2, :],
                                     w1_v[kind][:, 4 * j + 2 * h:4 * j + 2 * h + 2, :]).then_inc(done, 16)
                elif kind == "vsg":
                    v = raw[:, r % 4, 0:2 * VSG].rearrange("p (c n) -> p c n", c=2)
                    a, b = COL["v_slc"], COL["v_win"]
                    sp.dma_start(v[:, :, 0:P], w_in_v[:, 2 * j:2 * j + 2, a:a + P]).then_inc(done, 16)
                    sp.dma_start(v[:, :, P:VSG], w_in_v[:, 2 * j:2 * j + 2, b:b + VSG - P]).then_inc(done, 16)
                elif kind == "vb":
                    for h in range(2):
                        sp.dma_start(raw[:, r % 4, S * h:S * h + S],
                                     w_in_v[:, 2 * j + h, COL["v_b"]:COL["v_b"] + S]).then_inc(done, 16)
                else:
                    for h in range(2):
                        row = HD * (j + 4 * h) if j < NSA_PAIRS else P * j + HD * h
                        sp.dma_start(raw[HD * h:HD * h + HD, r % 4, :], w_out[row:row + HD, :]).then_inc(done, 16)

            for r in range(NW):
                if r == 1:
                    sp.wait_ge(x_load[NT - 1], 16)
                load_weights(r)
            sp.wait_ge(co_mm, 4)
            sp.dma_start(gpost, post_g.partition_broadcast(P)).then_inc(g_load, 16)
            sp.wait_ge(pv_done, 4 * NU)
            for t in range(NT):
                sp.dma_start(x_in[:, t, :], x_v[:, t, :]).then_inc(r_load, 16)
            for t in range(NT):
                sp.wait_ge(y_add, t + 1)
                sp.dma_start(out_v[:, t, :], y_out[:, t, :]).then_inc(y_out_s, 16)
            sp.wait_ge(y_out_s, 16 * NT)

        @block.gpsimd
        def _(pool):
            nc.gpsimd.memset(zf[:, 1344:2112], 0.0)
            nc.gpsimd.memset(kbd_h[:, :], 0.0)
            nc.gpsimd.memset(kbd_l[:, :], 0.0).then_inc(zeroed, 1)
            nc.gpsimd.memset(gw[:, 2 * NSA_PAIRS:NU, :, :], 1.0).then_inc(zeroed, 1)
            pool.wait_ge(table, 2)
            for n, r in enumerate(ropes):
                pool.wait_ge(t_evac, t_of[r] + 1)
                if n >= 2:
                    pool.wait_ge(rope_add, n - 1)
                nc.gpsimd.tensor_tensor(uu[:, n % 2, :], xf[:, n % 2, :], cos_t, ALU.mult).then_inc(rope_u, 1)

            def mixed(o):
                mx = mix[:, o % 2, :]
                if o < NSA_PAIRS:
                    pool.wait_ge(o_read, 2 * o + 2)
                    nc.gpsimd.tensor_tensor(mx, mx, zreg[:, o, :], ALU.mult).then_inc(mix_z, 1)
                pool.wait_ge(m_hi, o + 1)
                nc.gpsimd.tensor_tensor(r32(q_l[:, o, :]), mx, q_h[:, o, :], ALU.subtract).then_inc(m_lo, 1)

            for U in range(NU):
                for i in range(2):
                    qt = 3 - i
                    N = P * (qt + 1)
                    pool.wait_ge(w_ready, 4 * U + i + 1)
                    for a in range(2):
                        pa = prob[:, U % 2, a, off(qt):off(qt) + N]
                        last = nc.gpsimd.tensor_tensor(
                            pa, pa, rw[:, U % 2, qt, a:a + 1].to_broadcast([P, N]), ALU.mult)
                    last.then_inc(pn_g, 1)
                if U >= 2 and mixed_after(U - 2) is not None:
                    mixed(mixed_after(U - 2))
            mixed(PAIRS - 2)
            mixed(PAIRS - 1)

        @block.scalar
        def _(act):
            act.dma_start(posi, positions.rearrange("b s -> (b s)").partition_broadcast(P)).then_inc(p_load, 16)
            act.dma_start(cst[:, 0:C_CAUSAL], consts[:, 0:C_CAUSAL]).then_inc(c_load, 16)
            act.dma_start(grow, pre_g.rearrange("(c p) -> c p", p=P)).then_inc(k_load, 16)
            for i, (pos, w2) in enumerate(((ck_pos, ck_w2), (cv_pos, cv_w2))):
                for h in range(2):
                    act.dma_start(posr[i][:, HD * h:HD * h + HD], pos).then_inc(k_load, 16)
            w2v_k = ck_w2.rearrange("(j p) n -> p j n", p=P)
            for h in range(2):
                act.dma_start(w2k[:, :, HD * h:HD * h + HD], w2v_k).then_inc(k_load, 16)
            act.dma_start(w2v, cv_w2.rearrange("(j p) n -> p j n", p=P)).then_inc(k_load, 16)
            act.dma_start(cst[:, C_CAUSAL:C_END], consts[:, C_CAUSAL:C_END]).then_inc(t_load, 16)

            for t in range(NT):
                act.wait_ge(x_load[t], 16)
                if t:
                    act.wait_ge(ssq, t)
                nc.scalar.activation(xjunk, x_in[:, t, :], ACT.Square, accum_out=stat[:, t:t + 1]).then_inc(ssq, 1)
                act.wait_ge(var, t + 1)
                nc.scalar.activation(stat[:, 8 + t:9 + t], stat[:, 4 + t:5 + t], ACT.Sqrt).then_inc(std, 1)

            def split_high(r):
                act.wait_ge(w_load[r % 4], 32 * (r // 4 + 1))
                if r >= 2:
                    act.wait_ge(w_used, r - 1)
                n = width(r)
                nc.scalar.activation(r32(w_h[:, r % 2, 0:n]), raw[:, r % 4, 0:n], ACT.Copy).then_inc(w_hi, 1)

            split_high(0)
            for c in range(NC):
                act.wait_ge(x_tr, c + 1)
                if c == 0:
                    act.wait_ge(pos_cp, 3)
                nc.scalar.activation(r32(h_h[:, c, :]), ps[:, c, :], ACT.Copy, scale=gpre[:, c:c + 1])\
                    .then_inc(h_hi, 1)
            split_high(1)
            for i in range(2):
                act.wait_ge(angle, i + 1)
                nc.scalar.activation((sin_t, cos_t)[i], red[i], ACT.Sin).then_inc(table, 1)

            def evacuate(r):
                kind, base, how = tiles[r]
                t = t_of[r]
                act.wait_ge(w_used, r + 1)
                bank = ps[:, t % 2, :]
                if how == ROPE:
                    n = rho_of[r]
                    if n >= 2:
                        act.wait_ge(rotated, n - 1)
                        act.wait_ge(rope_u, n - 1)
                    nc.scalar.activation(xf[:, n % 2, :], bank, ACT.Copy).then_inc(t_evac, 1)
                elif how == COPY:
                    nc.scalar.activation(vc_t, bank, ACT.Copy).then_inc(t_evac, 1)
                else:
                    z = t - 16
                    if z == 0:
                        act.wait_ge(co_mm, 4)
                    nc.scalar.activation(zreg[:, z, :], bank, ACT.Silu).then_inc(t_evac, 1)

            def rope_high(n):
                act.wait_ge(rope_add, n + 1)
                nc.scalar.activation(r32(qk_slot(n)[0]), rr[:, n % 2, :], ACT.Copy).then_inc(rope_hi, 1)

            def values(v, r0):
                act.wait_ge(w_used, r0 + 4)
                bank = ps[:, 4 + v, :]
                if r0 == R_VSG:
                    nc.scalar.activation(v3[:, 0:4, v, 0, :], bank[:, 0:2 * P].rearrange("p (u d) -> p u d", u=4),
                                         ACT.Copy)
                    nc.scalar.activation(gates[:, v, :], bank[:, 2 * P:VSG], ACT.Copy).then_inc(v_hi, 1)
                else:
                    nc.scalar.activation(v3[:, 4:12, v, 0, :], bank.rearrange("p (u d) -> p u d", u=8),
                                         ACT.Copy).then_inc(v_hi, 1)

            for r in range(NPH):
                if r + 2 < NPH + 2:
                    split_high(r + 2)
                if r in t_of:
                    evacuate(r)
                if r - 1 in rho_of and rho_of[r - 1] >= 1:
                    rope_high(rho_of[r - 1])
                if r == 1:
                    act.wait_ge(f_built, 1)
                    nc.scalar.activation(r32(f_h[0]), f_tmp, ACT.Copy).then_inc(f_hid, 1)
                if r == 2:
                    act.wait_ge(f_built, 2)
                    nc.scalar.activation(r32(f_h[1]), f_tmp, ACT.Copy).then_inc(f_hid, 1)
                if r in (R_W1K + 6, R_W1V + 6):
                    i = 0 if r == R_W1K + 6 else 1
                    act.wait_ge(w_used, r + 1)
                    nc.scalar.activation(h1s[i], ps[0:2 * NB, 3, 0:CH], ACT.Silu).then_inc(h1_silu, 1)
                if r == R_VSG + 1:
                    act.wait_ge(c_mm, 1)
                    act.wait_ge(zeroed, 1)
                    for g in range(2):
                        rows = slice(HD * g, HD * g + HD)
                        last = nc.scalar.activation(r32(kbd_h[rows, CP * g:CP * g + NB]),
                                                    ps[rows, 3, 384 + NB * g:384 + NB * g + NB], ACT.Copy)
                    last.then_inc(c_hi, 1)
                if r in (R_VSG + 3, R_VB + 3):
                    for v in range(NT):
                        values(v, r - 3)
                    if r == R_VSG + 3:
                        act.wait_ge(v_hi, 4)
                        nc.scalar.activation(gates[:, :, :], gates[:, :, :], ACT.Exp, scale=-1.0)\
                            .then_inc(gate_e, 1)
                if r == R_KB:
                    act.wait_ge(cs_dve, 3)
                    nc.scalar.activation(cs, cs, ACT.Exp, scale=SCALE).then_inc(cs_exp, 1)
                if r == R_KB + 1:
                    for p in range(4):
                        act.wait_ge(cp_tr, p + 1)
                        nc.scalar.activation(pct[0:2 * CP, p, :], ps[0:2 * CP, 4 + p, :], ACT.Copy)\
                            .then_inc(cp_cp, 1)
                if r == R_KB + 2:
                    for p in range(4):
                        act.wait_ge(co_mm, p + 1)
                        nc.scalar.activation(oc[:, p, :], ps[:, 4 + p, :], ACT.Copy).then_inc(co_cp, 1)

            def exps(U, i):
                qt = 3 - i
                N = P * (qt + 1)
                for a in range(2):
                    act.wait_ge(s_masked, 8 * U + 2 * i + a + 1)
                    pa = prob[:, U % 2, a, off(qt):off(qt) + N]
                    nc.scalar.activation(pa, pa, ACT.Exp, bias=nmx[:, U % 2, qt, a:a + 1], scale=-1.0,
                                         accum_out=den[:, U % 2, qt, a:a + 1]).then_inc(p_exp, 1)

            def pt_high(U, i):
                N = P * (i + 1)
                for a in range(2):
                    m = (2 * i + a) % 4
                    act.wait_ge(pt_ready, 8 * U + 2 * i + a + 1)
                    if U:
                        act.wait_ge(pv_done, 4 * U + i - 3)
                    nc.scalar.activation(pt_h[:, a, off(i):off(i) + N], ps[:, 2 + m, 0:N], ACT.Copy).then_inc(pt_hi, 1)

            def mix_high(o):
                if o < NSA_PAIRS:
                    act.wait_ge(mix_z, o + 1)
                else:
                    act.wait_ge(o_read, o + NSA_PAIRS + 1)
                nc.scalar.activation(r32(q_h[:, o, :]), mix[:, o % 2, :], ACT.Copy).then_inc(m_hi, 1)

            for g in range(4):
                exps(0, g)
            for g in range(G):
                U, i = g // 4, g % 4
                if U + 1 < NU:
                    exps(U + 1, i)
                pt_high(U, i)
                if i == 3 and U >= 1 and mixed_after(U - 1) is not None:
                    mix_high(mixed_after(U - 1))
            mix_high(PAIRS - 1)
            for r in range(NPH + 2, NW):
                split_high(r)
            for t in range(NT):
                act.wait_ge(y_mm, t + 1)
                for h in range(2):
                    last = nc.scalar.activation(junk[:, S * h:S * h + S], ps[:, 2 * t + h, :], ACT.Square,
                                                accum_out=stat[:, 16 + 2 * t + h:17 + 2 * t + h])
                    last.then_inc(y_sq, 1)
                    act.wait_ge(y_sq, 2 * t + h + 1)
                act.wait_ge(y_var, t + 1)
                nc.scalar.activation(stat[:, 32 + t:33 + t], stat[:, 28 + t:29 + t], ACT.Sqrt).then_inc(y_std, 1)

        @block.vector
        def _(dve):
            V = nc.vector
            k = 0

            def link(ins):
                nonlocal k
                k += 1
                ins.then_inc(chain, 1)
                dve.wait_ge(chain, k)

            dve.wait_ge(pos_tr, 1)
            V.tensor_copy(gpre[:, :], ps[:, 7, 0:NC]).then_inc(pos_cp, 1)
            for i in range(2):
                V.tensor_copy(post[i], ps[:, 7, CL * (i + 1):CL * (i + 2)]).then_inc(pos_cp, 1)
            for t in range(NT):
                dve.wait_ge(ssq, t + 1)
                V.tensor_scalar(stat[:, 4 + t:5 + t], stat[:, t:t + 1], 1.0 / DM, EPS, ALU.mult, ALU.add)\
                    .then_inc(var, 1)
                dve.wait_ge(std, t + 1)
                link(V.reciprocal(stat[:, 12 + t:13 + t], stat[:, 8 + t:9 + t]))
                V.tensor_scalar(x_n[:, t, :], x_in[:, t, :], stat[:, 12 + t:13 + t], None, ALU.mult)\
                    .then_inc(xn_done, 1)

            def split_low(r):
                dve.wait_ge(w_hi, r + 1)
                n = width(r)
                V.tensor_tensor(r32(w_l[:, r % 2, 0:n]), raw[:, r % 4, 0:n], w_h[:, r % 2, 0:n], ALU.subtract)\
                    .then_inc(w_lo, 1)

            split_low(0)
            for c in range(NC):
                dve.wait_ge(h_hi, c + 1)
                V.scalar_tensor_tensor(r32(h_l[:, c, :]), ps[:, c, :], gpre[:, c:c + 1], h_h[:, c, :],
                                       ALU.mult, ALU.subtract).then_inc(h_lo, 1)
            split_low(1)
            dve.wait_ge(p_load, 16)
            dve.wait_ge(c_load, 16)
            link(V.tensor_copy(posf, posi))
            link(V.tensor_scalar(ang, posf, inv, None, ALU.mult))
            link(V.tensor_scalar(trn[0], ang, float(1 / TWO_PI), 0.0, ALU.mult, ALU.add))
            link(V.tensor_scalar(trn[1], ang, float(1 / TWO_PI), 0.25, ALU.mult, ALU.add))
            for i in range(2):
                link(V.tensor_scalar(trn[i], trn[i], ROUND, None, ALU.add))
                link(V.tensor_scalar(trn[i], trn[i], ROUND, None, ALU.subtract))
                link(V.scalar_tensor_tensor(red[i], trn[i], -TP1, ang, ALU.mult, ALU.add))
                link(V.scalar_tensor_tensor(red[i], trn[i], -TP2, red[i], ALU.mult, ALU.add))
                link(V.scalar_tensor_tensor(red[i], trn[i], -TP3, red[i], ALU.mult, ALU.add))
                if i:
                    link(V.tensor_scalar(red[i], red[i], float(np.pi / 2), None, ALU.add))
                V.tensor_scalar(red[i], red[i], PI_IN, -PI_IN, ALU.min, ALU.max).then_inc(angle, 1)

            def rope(n):
                dve.wait_ge(rotated, n + 1)
                if n:
                    dve.wait_ge(rope_add, n)
                V.tensor_tensor(tt, ps[:, 2, :], sin_t, ALU.mult).then_inc(rope_mul, 1)
                dve.wait_ge(rope_mul, n + 1)
                dve.wait_ge(rope_u, n + 1)
                if n >= 3:
                    dve.wait_ge(rope_hi, n - 2)
                    dve.wait_ge(rope_lo, n - 2)
                dst = rr[:, n % 2, :] if n else kc_t
                V.tensor_tensor(dst, tt, uu[:, n % 2, :], ALU.add).then_inc(rope_add, 1)
                if n:
                    dve.wait_ge(rope_hi, n)
                    hi, lo = qk_slot(n)
                    V.tensor_tensor(r32(lo), rr[:, n % 2, :], hi, ALU.subtract).then_inc(rope_lo, 1)

            def blocks(i):
                src = (kc_t, vc_t)[i]
                fv = f_tmp.rearrange("p (a j g c) -> p a j g c", a=2, j=8, g=2)
                if i:
                    dve.wait_ge(f_lod, 1)
                    dve.wait_ge(t_evac, 2)
                else:
                    dve.wait_ge(rope_add, 1)
                    dve.wait_ge(pos_cp, 3)
                for g in range(2):
                    rows = slice(HD * g, HD * g + HD)
                    sv_ = src[rows, :].rearrange("p (c j t) -> p t j c", j=8, t=2)
                    pv_ = post[i][rows, :].rearrange("p (a j t) -> p a t j", a=2, t=2)
                    for half in range(2):
                        for a in range(2):
                            last = V.tensor_tensor(
                                fv[HD * half:HD * half + HD, a, :, g, :],
                                sv_[:, half, :, a:a + NB],
                                pv_[:, a, half, :].unsqueeze(2).to_broadcast([HD, 8, NB]), ALU.add)
                last.then_inc(f_built, 1)
                dve.wait_ge(f_hid, i + 1)
                V.tensor_tensor(r32(f_l[i]), f_tmp, f_h[i], ALU.subtract).then_inc(f_lod, 1)

            def values_low(v, r0):
                vi = v + (4 if r0 == R_VB else 0)
                n, u0 = (2 * P, 0) if r0 == R_VSG else (S, 4)
                u1 = u0 + n // HD
                rest = vt[:, 0:n].rearrange("p (u d) -> p u d", d=HD)
                dve.wait_ge(v_hi, vi + 1)
                if vi:
                    dve.wait_ge(v_done, vi)
                V.tensor_tensor(rest, ps[:, 4 + v, 0:n].rearrange("p (u d) -> p u d", d=HD),
                                v3[:, u0:u1, v, 0, :], ALU.subtract).then_inc(v_rest, 1)
                dve.wait_ge(v_rest, vi + 1)
                V.tensor_copy(v3[:, u0:u1, v, 1, :], rest).then_inc(v_mid, 1)
                dve.wait_ge(v_mid, vi + 1)
                V.tensor_tensor(v3[:, u0:u1, v, 2, :], rest, v3[:, u0:u1, v, 1, :], ALU.subtract)\
                    .then_inc(v_done, 1)

            vt = tt
            for r in range(NPH):
                split_low(r + 2)
                if r - 1 in rho_of:
                    rope(rho_of[r - 1])
                if r in (1, 2):
                    blocks(r - 1)
                if r == R_VSG:
                    dve.wait_ge(h1_tr, 1)
                    V.tensor_copy(h1kt, ps[:, 3, CH:CH + 4 * NB].rearrange("p (j n) -> p j n", j=2)).then_inc(h1_cp, 1)
                if r == R_VSG + 1:
                    dve.wait_ge(c_hi, 1)
                    for g in range(2):
                        rows = slice(HD * g, HD * g + HD)
                        last = V.tensor_tensor(r32(kbd_l[rows, CP * g:CP * g + NB]),
                                               ps[rows, 3, 384 + NB * g:384 + NB * g + NB],
                                               kbd_h[rows, CP * g:CP * g + NB], ALU.subtract)
                    last.then_inc(c_lo, 1)
                if r == R_KB - 1:
                    dve.wait_ge(h1_tr, 2)
                    dve.wait_ge(zeroed, 1)
                    for j in range(2):
                        last = V.tensor_copy(h1vt[:, j, :, 0:NB],
                                             ps[:, 3, CH + 2 * NB * j:CH + 2 * NB * (j + 1)]
                                             .rearrange("p (g n) -> p g n", g=2))
                    last.then_inc(h1_cp, 1)
                if r == R_KB:
                    dve.wait_ge(c_mm, 2)
                    for g in range(2):
                        rows = slice(CP * g, CP * g + CP)
                        last = V.tensor_copy(vbd[rows, HD * g:HD * g + HD], ps[rows, 3, 448:512])
                    last.then_inc(c_lo, 1)
                if r in (R_VSG + 3, R_VB + 3):
                    for v in range(NT):
                        values_low(v, r - 3)
                    if r == R_VSG + 3:
                        dve.wait_ge(gate_e, 1)
                        link(V.tensor_scalar(gates[:, :, :], gates[:, :, :], 1.0, None, ALU.add))
                        link(V.reciprocal(gates[:, :, :], gates[:, :, :]))
                        gv = gates[:, :, :].rearrange("p t (b a q) -> p b a q t", b=3, a=2)
                        for b in range(2):
                            for a in range(2):
                                last = V.tensor_copy(gw[:, b:2 * NSA_PAIRS:2, :, a], gv[:, b + 1, a, :, :])
                        last.then_inc(gate_s, 1)
                if r == R_KB - 1:
                    dve.wait_ge(cs_mm, 1)
                    dve.wait_ge(t_load, 16)
                    for b in range(2):
                        sc = ps[:, 4 + b, :].rearrange("p (t h c) -> p t h c", t=2, h=8)
                        last = V.tensor_tensor(cs[:, 2 * b:2 * b + 2, :, :], sc,
                                               cadd[:, 2 * b:2 * b + 2, :].unsqueeze(2).to_broadcast([P, 2, 8, CP]),
                                               ALU.add)
                    last.then_inc(cs_dve, 1)
                    dve.wait_ge(cs_dve, 1)
                    csf = cs.rearrange("p t h c -> p (t h) c")
                    V.tensor_reduce(cden[:, 0, :], csf, AX, ALU.max).then_inc(cs_dve, 1)
                    dve.wait_ge(cs_dve, 2)
                    V.tensor_tensor(csf, csf, cden[:, 0, :].unsqueeze(2).to_broadcast([P, NT * 8, CP]),
                                    ALU.subtract).then_inc(cs_dve, 1)
                if r == R_KB:
                    dve.wait_ge(cs_exp, 1)
                    csf = cs.rearrange("p t h c -> p (t h) c")
                    link(V.tensor_tensor(cs, cs, cval.unsqueeze(2).to_broadcast([P, NT, 8, CP]), ALU.mult))
                    link(V.tensor_reduce(cden[:, 0, :], csf, AX, ALU.add))
                    link(V.tensor_scalar(cden[:, 1, :], cden[:, 0, :], 1e-30, None, ALU.max))
                    link(V.reciprocal(cden[:, 2, :], cden[:, 1, :]))
                    link(V.tensor_tensor(cden[:, 1, :].rearrange("p (t q a) -> p t q a", t=NT, a=2),
                                         cden[:, 2, :].rearrange("p (t q a) -> p t q a", t=NT, a=2),
                                         gates[:, :, 0:8].rearrange("p t (a q) -> p t q a", a=2), ALU.mult))
                    V.tensor_tensor(csf, csf, cden[:, 1, :].unsqueeze(2).to_broadcast([P, NT * 8, CP]),
                                    ALU.mult).then_inc(cs_dve, 1)

            def mask(U, i):
                qt = 3 - i
                N = P * (qt + 1)
                bias = causal if U < 2 * NSA_PAIRS else dilated
                dve.wait_ge(s_ready, 4 * U + i + 1)
                if i == 0 and U >= 2:
                    dve.wait_ge(pt_ready, 8 * (U - 1))
                for a in range(2):
                    V.tensor_tensor_reduce(out=prob[:, U % 2, a, off(qt):off(qt) + N], in0=ps[:, a, 0:N],
                                           in1=bias[:, S - N:S], scale=-SCALE, scalar=BIG, op0=ALU.add,
                                           op1=ALU.min, accum_out=nmx[:, U % 2, qt, a:a + 1]).then_inc(s_masked, 1)

            def weigh(U, i):
                qt = 3 - i
                n = 4 * U + i
                dve.wait_ge(p_exp, 2 * n + 2)
                if i == 0 and U >= 2:
                    dve.wait_ge(pn_g, 2 * (U - 1))
                V.reciprocal(rw[:, U % 2, qt, :], den[:, U % 2, qt, :]).then_inc(p_rec, 1)
                dve.wait_ge(p_rec, n + 1)
                V.tensor_tensor(rw[:, U % 2, qt, :], rw[:, U % 2, qt, :], gw[:, U, qt, :], ALU.mult)\
                    .then_inc(w_ready, 1)
                if qt < 2:
                    dve.wait_ge(w_ready, n + 1)
                    N = P * (qt + 1)
                    for a in range(2):
                        pa = prob[:, U % 2, a, off(qt):off(qt) + N]
                        last = V.tensor_scalar(pa, pa, rw[:, U % 2, qt, a:a + 1], None, ALU.mult)
                    last.then_inc(pn_v, 1)

            def pt_low(U, i):
                N = P * (i + 1)
                for a in range(2):
                    m = (2 * i + a) % 4
                    dve.wait_ge(pt_hi, 8 * U + 2 * i + a + 1)
                    c = slice(off(i), off(i) + N)
                    V.tensor_tensor(pt_l[:, a, c], ps[:, 2 + m, 0:N], pt_h[:, a, c], ALU.subtract)\
                        .then_inc(pt_lo, 1)

            def collect(U):
                dve.wait_ge(pv_done, 4 * U + 4)
                bank = ps[:, 6 + U % 2, :]
                if U < 2 * NSA_PAIRS:
                    p = U // 2
                    mx = mix[:, p % 2, :]
                    if U % 2 == 0:
                        if p >= 2:
                            dve.wait_ge(m_hi, p - 1)
                            dve.wait_ge(m_lo, p - 1)
                        if p == 0:
                            dve.wait_ge(co_cp, 4)
                        V.tensor_tensor(mx, bank, oc[:, p, :], ALU.add).then_inc(o_read, 1)
                    else:
                        dve.wait_ge(o_read, U)
                        V.tensor_tensor(mx, bank, mx, ALU.add).then_inc(o_read, 1)
                else:
                    o = U - NSA_PAIRS
                    dve.wait_ge(m_hi, o - 1)
                    dve.wait_ge(m_lo, o - 1)
                    V.tensor_tensor(mix[:, o % 2, :], bank, zreg[:, o, :], ALU.mult).then_inc(o_read, 1)

            dve.wait_ge(w_used, NPH)
            dve.wait_ge(zeroed, 2)
            dve.wait_ge(gate_s, 1)
            for i in range(NT):
                mask(0, i)
                if i:
                    weigh(0, i - 1)
            for g in range(G):
                U, i = g // 4, g % 4
                if U + 1 < NU:
                    mask(U + 1, i)
                if g:
                    pt_low((g - 1) // 4, (g - 1) % 4)
                if g + 3 < G:
                    weigh((g + 3) // 4, (g + 3) % 4)
                if i == 2 and U >= 1:
                    collect(U - 1)
            pt_low(NU - 1, NT - 1)
            collect(NU - 1)
            for r in range(NPH + 2, NW):
                split_low(r)
            dve.wait_ge(g_load, 16)
            dve.wait_ge(r_load, 16 * NT)
            for t in range(NT):
                dve.wait_ge(y_sq, 2 * t + 2)
                link(V.tensor_tensor(stat[:, 24 + t:25 + t], stat[:, 16 + 2 * t:17 + 2 * t],
                                     stat[:, 17 + 2 * t:18 + 2 * t], ALU.add))
                V.tensor_scalar(stat[:, 28 + t:29 + t], stat[:, 24 + t:25 + t], 1.0 / DM, EPS, ALU.mult, ALU.add)\
                    .then_inc(y_var, 1)
                dve.wait_ge(y_std, t + 1)
                link(V.reciprocal(stat[:, 36 + t:37 + t], stat[:, 32 + t:33 + t]))
                for h in range(2):
                    last = V.scalar_tensor_tensor(y_out[:, t, S * h:S * h + S], ps[:, 2 * t + h, :],
                                                  stat[:, 36 + t:37 + t], gpost[:, S * h:S * h + S],
                                                  ALU.mult, ALU.mult)
                last.then_inc(y_mul, 1)
                dve.wait_ge(y_mul, t + 1)
                V.tensor_tensor(y_out[:, t, :], y_out[:, t, :], x_in[:, t, :], ALU.add).then_inc(y_add, 1)

        @block.tensor
        def _(pe):
            T = nc.tensor
            pe.wait_ge(c_load, 16)
            pe.wait_ge(k_load, 16 * 8)
            T.transpose(ps[:, 7, 0:NC], grow, ident[0:NC, 0:NC])
            for i in range(2):
                last = T.transpose(ps[:, 7, CL * (i + 1):CL * (i + 2)], posr[i], ident[0:CL, 0:CL])
            last.then_inc(pos_tr, 1)
            for t in range(NT):
                pe.wait_ge(xn_done, t + 1)
                for c in range(NC):
                    if t == 0 and c == NC - 1:
                        pe.wait_ge(pos_cp, 3)
                    last = T.transpose(ps[:, c, P * t:P * t + P], x_n[:, t, P * c:P * c + P], ident)
                    if t == NT - 1:
                        last.then_inc(x_tr, 1)

            def three(dst, lh, ll, rh, rl, first, last):
                T.matmul(dst, r32(lh), r32(rh), start=first, stop=False)
                T.matmul(dst, r32(ll), r32(rh), start=False, stop=False)
                return T.matmul(dst, r32(lh), r32(rl), start=False, stop=last)

            def main(r):
                kind, j, how = tiles[r]
                pe.wait_ge(w_lo, r + 1)
                wh, wl = w_h[:, r % 2, :], w_l[:, r % 2, :]
                if kind in ("proj", "pair"):
                    t = t_of[r]
                    if t >= 2:
                        pe.wait_ge(t_evac, t - 1)
                    for c in range(NC):
                        if t == 0:
                            pe.wait_ge(h_lo, NC if c == 0 else NC)
                        cc = slice(P * c, P * c + P)
                        last = three(ps[:, t % 2, :], wh[:, cc], wl[:, cc], h_h[:, c, :], h_l[:, c, :],
                                     c == 0, c == NC - 1)
                elif kind in ("w1k", "w1v"):
                    i = 0 if kind == "w1k" else 1
                    if j == 0:
                        pe.wait_ge(f_lod, i + 1)
                        if i:
                            pe.wait_ge(c_lo, 1)
                    for jj in range(4):
                        st = 4 * j + jj
                        fc = slice(2 * NB * st, 2 * NB * (st + 1))
                        wc = slice(CH * jj, CH * jj + CH)
                        last = three(ps[0:2 * NB, 3, 0:CH], f_h[i][:, fc], f_l[i][:, fc], wh[:, wc], wl[:, wc],
                                     st == 0, st == 15)
                elif kind in ("vsg", "vb"):
                    N = VSG if kind == "vsg" else S
                    if kind == "vb" and j == 0:
                        pe.wait_ge(co_cp, 4)
                    for t in range(NT):
                        tc = slice(P * t, P * t + P)
                        for jj in range(2):
                            c = 2 * j + jj
                            wc = slice(N * jj, N * jj + N)
                            last = three(ps[:, 4 + t, 0:N], h_h[:, c, tc], h_l[:, c, tc], wh[:, wc], wl[:, wc],
                                         c == 0, c == NC - 1)
                last.then_inc(w_used, 1)

            def rotate(n):
                pe.wait_ge(t_evac, t_of[ropes[n]] + 1)
                if n:
                    pe.wait_ge(rope_mul, n)
                T.matmul(ps[:, 2, :], rot, xf[:, n % 2, :], start=True, stop=True).then_inc(rotated, 1)

            for r in range(NPH):
                main(r)
                if r - 1 in rho_of:
                    rotate(rho_of[r - 1])
                if r in (R_VSG, R_KB - 1):
                    i = 0 if r == R_VSG else 1
                    pe.wait_ge(h1_silu, i + 1)
                    for j in range(2):
                        last = T.transpose(ps[:, 3, CH + 2 * NB * j:CH + 2 * NB * (j + 1)],
                                           h1s[i][:, P * j:P * j + P], ident[0:2 * NB, 0:2 * NB])
                    last.then_inc(h1_tr, 1)
                if r == R_VSG + 1:
                    pe.wait_ge(h1_cp, 1)
                    for j in range(2):
                        last = T.matmul(ps[:, 3, 384:384 + 2 * NB], w2k[:, j, :], h1kt[:, j, :],
                                        start=j == 0, stop=j == 1)
                    last.then_inc(c_mm, 1)
                if r == R_KB:
                    pe.wait_ge(h1_cp, 2)
                    for j in range(2):
                        last = T.matmul(ps[0:2 * CP, 3, 448:512], h1vt[:, j, :, :].rearrange("p g n -> p (g n)"),
                                        w2v[:, j, :], start=j == 0, stop=j == 1)
                    last.then_inc(c_mm, 1)
                if r in (R_QB, R_QB + 2, R_QB + 4, R_QB + 6):
                    t = (r - R_QB) // 2
                    if t == 0:
                        pe.wait_ge(v_done, 4)
                        pe.wait_ge(rope_lo, 6)
                    for p in range(4):
                        tc = slice(P * t, P * t + P)
                        o = 256 * (t % 2) + 64 * p
                        last = three(ps[:, 4 + t // 2, o:o + 64], q_h[:, p, tc], q_l[:, p, tc],
                                     kbd_h[:, :], kbd_l[:, :], True, True)
                    if t == NT - 1:
                        last.then_inc(cs_mm, 1)
                if r == R_KB + 1:
                    pe.wait_ge(cs_dve, 4)
                    for p in range(4):
                        for t in range(NT):
                            last = T.transpose(ps[0:2 * CP, 4 + p, P * t:P * t + P],
                                               cs[:, t, 2 * p:2 * p + 2, :].rearrange("p h c -> p (h c)"), ident)
                        last.then_inc(cp_tr, 1)
                if r == R_KB + 2:
                    pe.wait_ge(c_lo, 2)
                    for p in range(4):
                        pe.wait_ge(cp_cp, p + 1)
                        T.matmul(ps[:, 4 + p, :], vbd, pct[0:2 * CP, p, :], start=True, stop=True)\
                            .then_inc(co_mm, 1)

            def scores(U, i):
                qt = 3 - i
                N = max(P * (qt + 1), 2 * P)
                p, kk, _ = unit(U)
                if 4 * U + i >= 1:
                    pe.wait_ge(s_masked, 8 * U + 2 * i)
                for ql, kr in ((q_h, k_h), (q_l, k_h), (q_h, k_l)):
                    for a in range(2):
                        rows = slice(HD * a, HD * a + HD)
                        last = T.matmul(ps[:, a, 0:N], r32(ql[rows, p, P * qt:P * qt + P]), r32(kr[rows, kk, 0:N]),
                                        start=ql is q_h and kr is k_h, stop=kr is k_l)
                last.then_inc(s_ready, 1)

            def transposes(U, i):
                kt = 3 - i
                if kt >= 2:
                    pe.wait_ge(pn_g, 2 * U + i + 1)
                else:
                    pe.wait_ge(pn_v, 2 * U + i - 1)
                for a in range(2):
                    n = 8 * U + 2 * i + a
                    m = (2 * i + a) % 4
                    if n >= 4:
                        pe.wait_ge(pt_lo, n - 3)
                    for qt in range(kt, NT):
                        src = prob[:, U % 2, a, off(qt) + P * kt:off(qt) + P * kt + P]
                        last = T.transpose(ps[:, 2 + m, P * (qt - kt):P * (qt - kt) + P], src, ident)
                    last.then_inc(pt_ready, 1)

            def outputs(U, i):
                kt = 3 - i
                vu = unit(U)[2]
                pe.wait_ge(pt_lo, 8 * U + 2 * i + 2)
                if i == 0 and U >= 2:
                    pe.wait_ge(o_read, U - 1)
                N = P * (i + 1)
                for part, pt in ((0, pt_h), (1, pt_h), (2, pt_h), (0, pt_l), (1, pt_l)):
                    for a in range(2):
                        src = pt[:, a, off(i):off(i) + N]
                        dst = ps[HD * a:HD * a + HD, 6 + U % 2, P * kt:S]
                        first = part == 0 and pt is pt_h
                        for c in ((slice(0, P), slice(P, N)) if first and i else (slice(0, N),)):
                            last = T.matmul(dst[:, c], v3[:, vu + a, kt, part, :], src[:, c],
                                            start=first and i == 0, stop=i == 3 and part == 1 and pt is pt_l)
                last.then_inc(pv_done, 1)

            pe.wait_ge(rope_lo, len(ropes) - 1)
            pe.wait_ge(t_evac, len(proj))
            pe.wait_ge(v_done, 2 * NT)
            for i in range(NT):
                scores(0, i)
            for g in range(G + 2):
                U, i = g // 4, g % 4
                if U + 1 < NU:
                    scores(U + 1, i)
                if g < G:
                    transposes(U, i)
                if g >= 2:
                    outputs((g - 2) // 4, (g - 2) % 4)

            pe.wait_ge(o_read, NU)
            for o in range(PAIRS):
                r = NPH + o
                pe.wait_ge(w_lo, r + 1)
                pe.wait_ge(m_lo, o + 1)
                for t in range(NT):
                    tc = slice(P * t, P * t + P)
                    for h in range(2):
                        hc = slice(S * h, S * h + S)
                        last = three(ps[:, 2 * t + h, :], q_h[:, o, tc], q_l[:, o, tc], w_h[:, r % 2, hc],
                                     w_l[:, r % 2, hc], o == 0, o == PAIRS - 1)
                    if o == PAIRS - 1:
                        last.then_inc(y_mm, 1)
                if o < PAIRS - 1:
                    last.then_inc(w_used, 1)


def constants():
    c = np.zeros((P, C_END), np.float32)
    c[:, C_ID:C_ID + P] = np.eye(P)
    half = HD // 8
    for base in (0, HD):
        for i in range(half):
            c[base + half + i, C_ROT + base + i] = -1.0
            c[base + i, C_ROT + base + half + i] = 1.0
    inv = np.float32(1.0) / (np.float32(500000.0) ** (np.arange(0, 2 * half, 2, dtype=np.float32) / np.float32(2 * half)))
    for base in (0, half, HD, HD + half):
        c[base:base + half, C_INV] = inv
    i = np.arange(P)[:, None]
    dist = i + 3 * P - np.arange(S)[None, :]
    c[:, C_CAUSAL:C_CAUSAL + S] = np.where(dist >= 0, 0.0, NEG)
    count = ((dist <= 128).astype(int) + (dist % 4 == 0) + (dist % 16 == 0)) * (dist >= 0)
    c[:, C_DIL:C_DIL + S] = np.where(count > 0, np.log(np.maximum(count, 1)) / SCALE, NEG)
    tok = np.arange(P)[:, None, None] + P * np.arange(NT)[None, :, None]
    blk = np.arange(CP)[None, None, :]
    ok = (blk < NB) & (CS * blk + CL - 1 <= tok)
    c[:, C_CADD:C_CVAL] = np.where(ok, 0.0, NEG).reshape(P, -1)
    c[:, C_CVAL:C_END] = ok.reshape(P, -1)
    return c


def kernel(**inputs):
    import concourse.bacc as _bacc
    from concourse.bass_utils import run_bass_kernel_spmd as _run

    nc = _bacc.Bacc("TRN2", target_bir_lowering=False, num_devices=1)
    arrays, args = {}, []
    names = ["x", "positions", "pre_norm_g", "w_in", "cmp_k_pos", "cmp_k_w1", "cmp_k_w2", "cmp_v_pos", "cmp_v_w1",
             "cmp_v_w2", "w_out", "post_norm_g"]
    for name in names:
        a = np.ascontiguousarray(inputs[name])
        if name not in ("x", "positions"):
            a = a[0]
        arrays[f"in_{name}"] = np.ascontiguousarray(a)
    arrays["in_consts"] = constants()
    for name, a in arrays.items():
        args.append(nc.dram_tensor(name, a.shape, mybir.dt.from_np(a.dtype), kind="ExternalInput").ap())
    args.append(nc.dram_tensor("out_0", (1, S, DM), F32, kind="ExternalOutput").ap())
    hymba_kernel(nc, *args)
    r = _run(nc, [arrays], core_ids=[0])
    return r.results[0]["out_0"]
```

```python
from contextlib import ExitStack

import numpy as np

import concourse.bass as bass
from concourse import mybir

ALU = mybir.AluOpType
ACT = mybir.ActivationFunctionType
AX = mybir.AxisListType.X
F32 = mybir.dt.float32
F32R = mybir.dt.float32r
F16 = mybir.dt.float16
BF16 = mybir.dt.bfloat16
I32 = mybir.dt.int32

P = 128
S = 512
DM = 1024
HD = 64
NT = S // P
NC = DM // P
NSA_PAIRS = 4
DIL_PAIRS = 4
PAIRS = NSA_PAIRS + DIL_PAIRS
CL, CS, CH = 32, 16, 256
NB = (S - CL) // CS + 1
CP = 32
EPS = 1e-6
SCALE = HD ** -0.5
NEG = -1e30
BIG = 3e38

COL = dict(q_a=0, k_cmp=512, v_cmp=640, k_slc=768, v_slc=896, k_win=1024, v_win=1152, gate=1280,
           z_a=1304, q_b=1816, k_b=2328, v_b=2840, z_b=3352)
NG = 24
VSG = 2 * P + NG

C_ID, C_INV = 0, P
NF = HD // 4
C_CAUSAL = C_INV + NF
C_DIL = C_CAUSAL + S
C_CADD = C_DIL + S
C_CVAL = C_CADD + NT * CP
C_END = C_CVAL + NT * CP

TWO_PI = 2 * np.pi
TP1 = 6.28125
TP2 = float(np.round((TWO_PI - TP1) * 2 ** 20) / 2 ** 20)
TP3 = float(np.float32(TWO_PI - TP1 - TP2))
ROUND = 1.5 * 2 ** 23
PI_IN = 3.1415925

ROPE, COPY, SILU = "rope", "copy", "silu"


def weight_tiles():
    tiles = [("proj", COL[name], how)
             for name, how in (("k_cmp", ROPE), ("v_cmp", COPY), ("k_slc", ROPE), ("k_win", ROPE))]
    for j in range(4):
        tiles += [("pair", COL["q_a"] + HD * j, ROPE), ("w1k", j, None)]
    tiles += [("vsg", j, None) for j in range(4)]
    for j in range(4):
        tiles += [("w1v", j, None), ("proj", COL["q_b"] + P * j, ROPE)]
    tiles += [("proj", COL["k_b"] + P * j, ROPE) for j in range(4)]
    tiles += [("pair", COL["z_a"] + HD * j, SILU) for j in range(2)]
    tiles += [("vb", j, None) for j in range(4)]
    tiles += [("pair", COL["z_a"] + HD * j, SILU) for j in range(2, 4)]
    tiles += [("proj", COL["z_b"] + P * j, SILU) for j in range(4)]
    tiles += [("out", j, None) for j in range(8)]
    return tiles




def hymba_kernel(nc, x, positions, pre_g, w_in, ck_pos, ck_w1, ck_w2, cv_pos, cv_w1, cv_w2, w_out, post_g,
                 consts, out):
    tiles = weight_tiles()
    NW = len(tiles)
    NPH = NW - 12
    NZ = 4
    ZP = 8
    proj = [r for r in range(NW) if tiles[r][0] in ("proj", "pair")]
    t_of = {r: t for t, r in enumerate(proj)}
    NPRE = len(proj) - NZ
    ropes = [r for r in proj if tiles[r][2] == ROPE]
    rho_of = {r: n for n, r in enumerate(ropes)}
    R_VSG, R_VB, R_W1K, R_W1V = (tiles.index((kind, 0, None)) for kind in ("vsg", "vb", "w1k", "w1v"))
    R_QB = tiles.index(("proj", COL["q_b"], ROPE))
    R_KB = tiles.index(("proj", COL["k_b"], ROPE))
    G = 4 * (2 * NSA_PAIRS + DIL_PAIRS)

    ctx = ExitStack()
    with ctx:
        def sb(name, shape, dt=F32):
            return ctx.enter_context(nc.sbuf_tensor(name, shape, dt))

        def sem(name):
            return ctx.enter_context(nc.semaphore(name))

        def r32(ap):
            return ap.bitcast(F32R)

        cst = sb("cst", [P, C_END])
        ident = cst[:, C_ID:C_ID + P]
        inv = cst[:, C_INV:C_INV + NF]
        causal = cst[:, C_CAUSAL:C_CAUSAL + S]
        dilated = cst[:, C_DIL:C_DIL + S]
        cadd = cst[:, C_CADD:C_CADD + NT * CP].rearrange("p (t c) -> p t c", t=NT)
        cval = cst[:, C_CVAL:C_CVAL + NT * CP].rearrange("p (t c) -> p t c", t=NT)
        raw = sb("raw", [P, 4, DM])
        w_h = sb("w_h", [P, 2, DM])
        w_l = sb("w_l", [P, 2, DM])
        q_l = sb("q_l", [P, PAIRS, S])
        k_h = sb("k_h", [P, 2 + DIL_PAIRS, S])
        k_l = sb("k_l", [P, 2 + DIL_PAIRS, S])
        zreg = sb("zreg", [P, PAIRS, S])
        vreg = sb("vreg", [P, 12 * NT * 3 * HD // 2])
        v3 = vreg[:, :].bitcast(BF16).rearrange("p (u k s d) -> p u k s d", u=12, k=NT, s=3)
        x_in = vreg[:, 0:NT * DM].rearrange("p (t n) -> p t n", t=NT)
        gpre = sb("gpre", [P, NC])
        stat = sb("stat", [P, 64])
        gates = sb("gates", [P, NT, NG])
        gw = sb("gw", [P, 12, NT, 2])
        den = sb("den", [P, 2, NT, 2])
        nmx = sb("nmx", [P, 2, NT, 2])
        rw = sb("rw", [P, 2, NT, 2])
        cden = sb("cden", [P, 3, NT * 8])

        def overlay(*specs):
            with ExitStack() as own:
                return [own.enter_context(nc.sbuf_tensor(n, [P, w], F32))[:, :] for n, w in specs]

        x_n, = overlay(("x_n", NT * DM))
        x_n = x_n.rearrange("p (t n) -> p t n", t=NT)
        q_h = sb("q_h", [P, PAIRS, S])

        h_h, h_l = (t.rearrange("p (c s) -> p c s", c=NC) for t in overlay(("h_h", NC * S), ("h_l", NC * S)))
        y_out, junk, gpost = overlay(("y_out", NT * DM), ("junk", DM), ("gpost", DM))
        y_out = y_out.rearrange("p (t n) -> p t n", t=NT)
        sb("first_area", [P, 2 * NC * S])

        zhalf = sb("zhalf", [P, S])[:, :]

        FW = 16 * 2 * NB
        fkh, fkl, fvh, fvl, _, f_tmp, kc_t, vc_t, xf, xs, vt, rr, cos_t, sin_t = overlay(
            ("fkh", FW), ("fkl", FW), ("fvh", FW), ("fvl", FW), ("gap", 4 * (1024 - FW)), ("f_tmp", 1024),
            ("kc_t", S), ("vc_t", S), ("xf", 2 * S), ("xs", 2 * S), ("vt", S), ("rr", 2 * S),
            ("cos_t", S), ("sin_t", S))
        f_h, f_l = (fkh, fvh), (fkl, fvl)
        f_tmp = f_tmp[:, 0:FW]
        xf, xs, rr = (t.rearrange("p (b s) -> p b s", b=2) for t in (xf, xs, rr))
        oc, pct, cs = overlay(("oc", 4 * S), ("pct", 4 * S), ("cs", NT * 8 * CP))
        oc = oc.rearrange("p (a s) -> p a s", a=4)
        pct = pct.rearrange("p (a s) -> p a s", a=4)
        cs = cs.rearrange("p (t h c) -> p t h c", t=NT, h=8)
        PW = 1280
        _, prob, pt_h, pt_l, mix = overlay(("gap2", 4 * S), ("prob", 4 * PW), ("pt_h", PW), ("pt_l", PW),
                                           ("mix", 2 * S))
        prob = prob.rearrange("p (u a n) -> p u a n", u=2, a=2)
        pt_h = pt_h.bitcast(F16).rearrange("p (a n) -> p a n", a=2)
        pt_l = pt_l.bitcast(F16).rearrange("p (a n) -> p a n", a=2)
        mix = mix.rearrange("p (m n) -> p m n", m=2)
        SECOND = 4 * S + 6 * PW + 2 * S
        startup, = overlay(("startup", SECOND))
        sb("second_area", [P, SECOND])
        posi = startup[0:NT, 0:P].bitcast(I32)
        posf = startup[0:NT, P:2 * P]
        ang = startup[:, 256:256 + NT * NF].rearrange("p (t f) -> p t f", t=NT)
        trn = startup[:, 512:512 + 2 * NT * NF].rearrange("p (i t f) -> p i t f", i=2, t=NT)
        red = startup[:, 768:768 + 2 * NT * NF].rearrange("p (i t f) -> p i t f", i=2, t=NT)
        tok = startup[:, 1024:1024 + 2 * S].rearrange("p (i t a d) -> p i t a d", i=2, t=NT, a=2)
        xjunk = startup[:, 5632:5632 + DM]
        zf = zreg[:, :, :].rearrange("p a s -> p (a s)")
        w2k = zf[:, 0:256].rearrange("p (j n) -> p j n", j=2)
        w2v = zf[:, 256:384].rearrange("p (j n) -> p j n", j=2)
        posr = [zf[0:CL, 384 + 128 * i:512 + 128 * i] for i in range(2)]
        grow = zf[0:NC, 2112:2240]
        post = [zf[:, 640 + 32 * i:672 + 32 * i] for i in range(2)]
        h1s = [zf[0:2 * NB, 704 + 256 * i:960 + 256 * i] for i in range(2)]
        h1kt = zf[:, 1216:1216 + 4 * NB].rearrange("p (j n) -> p j n", j=2)
        h1vt = zf[:, 1344:1472].rearrange("p (j g n) -> p j g n", j=2, g=2)
        kbd_h = sb("kbd_h", [P, 2 * CP])
        kbd_l = sb("kbd_l", [P, 2 * CP])
        vbd = zf[0:2 * CP, 1856:1856 + P]

        ps = ctx.enter_context(nc.psum_tensor("ps", [P, 8, S], F32))

        x_load = [sem(f"x_load{t}") for t in range(NT)]
        w_load = [sem(f"w_load{slot}") for slot in range(4)]
        p_load, c_load, t_load = sem("p_load"), sem("c_load"), sem("t_load")
        k_load, g_load, r_load = sem("k_load"), sem("g_load"), sem("r_load")
        w_hi, w_lo, w_used = sem("w_hi"), sem("w_lo"), sem("w_used")
        ssq, var, std, xn_done = sem("ssq"), sem("var"), sem("std"), sem("xn_done")
        x_tr, h_hi, h_lo = sem("x_tr"), sem("h_hi"), sem("h_lo")
        pos_f, angle, tok_set = sem("pos_f"), sem("angle"), sem("tok_set")
        table_tok, table_tr, table = sem("table_tok"), sem("table_tr"), sem("table")
        pos_tr, pos_cp = sem("pos_tr"), sem("pos_cp")
        zeroed, xs_zero = sem("zeroed"), sem("xs_zero")
        t_evac = sem("t_evac")
        swapped = [sem(f"swapped{slot}") for slot in range(2)]
        rope_u, rope_mul, rope_add = sem("rope_u"), sem("rope_mul"), sem("rope_add")
        rope_hi, rope_lo = sem("rope_hi"), sem("rope_lo")
        f_built, f_hi_done, f_lo_done = sem("f_built"), sem("f_hi_done"), sem("f_lo_done")
        h1_silu, h1_tr, h1_cp = sem("h1_silu"), sem("h1_tr"), sem("h1_cp")
        c_mm, c_hi, c_lo = sem("c_mm"), sem("c_hi"), sem("c_lo")
        v_hi, v_rest, v_mid, v_done = sem("v_hi"), sem("v_rest"), sem("v_mid"), sem("v_done")
        gate_exp, gates_ready = sem("gate_exp"), sem("gates_ready")
        cs_mm, cs_dve, cs_exp = sem("cs_mm"), sem("cs_dve"), sem("cs_exp")
        cp_tr, cp_cp, co_mm, co_cp = sem("cp_tr"), sem("cp_cp"), sem("co_mm"), sem("co_cp")
        s_ready, s_masked, p_exp = sem("s_ready"), sem("s_masked"), sem("p_exp")
        p_rec, w_ready, pn_v, pn_g = sem("p_rec"), sem("w_ready"), sem("pn_v"), sem("pn_g")
        pt_ready, pt_hi, pt_lo, pv_done = sem("pt_ready"), sem("pt_hi"), sem("pt_lo"), sem("pv_done")
        z_mul, z_silu = sem("z_mul"), sem("z_silu")
        o_read, mix_z, m_hi, m_lo = sem("o_read"), sem("mix_z"), sem("m_hi"), sem("m_lo")
        y_mm, y_sq, y_var, y_std, y_mul = sem("y_mm"), sem("y_sq"), sem("y_var"), sem("y_std"), sem("y_mul")
        y_add_v, y_add_g, y_stored = sem("y_add_v"), sem("y_add_g"), sem("y_stored")
        chain = sem("chain")

        w_in_v = w_in.rearrange("(c p) n -> p c n", p=P)
        w1_v = {"w1k": ck_w1.rearrange("(j p) n -> p j n", p=P), "w1v": cv_w1.rearrange("(j p) n -> p j n", p=P)}
        x_v = x.rearrange("b (t p) n -> p (b t) n", p=P)
        out_v = out.rearrange("b (t p) n -> p (b t) n", p=P)

        def off(qt):
            return P * qt * (qt + 1) // 2

        def rotated_at(step):
            for r in (step - 1, step - 2):
                if r in rho_of:
                    late = tiles[r + 1][0] in ("w1k", "w1v")
                    if step - r == (2 if late else 1):
                        return rho_of[r]
            return None

        def halves(r):
            n = VSG if tiles[r][0] == "vsg" else DM // 2
            return slice(0, n), slice(n, 2 * n)

        def unit(U):
            if U < 2 * NSA_PAIRS:
                return U // 2, U % 2, 2 * (U % 2)
            i = U - 2 * NSA_PAIRS
            return NSA_PAIRS + i, 2 + i, 4 + 2 * i

        def qk_slot(n):
            if n < 3:
                return k_h[:, n - 1, :], k_l[:, n - 1, :]
            if n < 11:
                return q_h[:, n - 3, :], q_l[:, n - 3, :]
            return k_h[:, n - 9, :], k_l[:, n - 9, :]

        def mixed_after(U):
            if U < 2 * NSA_PAIRS:
                return U // 2 if U % 2 else None
            return U - NSA_PAIRS

        NU = 2 * NSA_PAIRS + DIL_PAIRS
        UZ = ZP * (NZ - 1) // 4

        def s_bank(U, i, a):
            return a if U <= UZ else (0, 1, 7)[(8 * (U - UZ - 1) + 2 * i + a) % 3]

        block = ctx.enter_context(nc.Block())

        @block.sync
        def _(sp):
            for t in range(NT):
                sp.dma_start(x_in[:, t, :], x_v[:, t, :]).then_inc(x_load[t], 16)

            def load_weights(r):
                kind, j, _ = tiles[r]
                done = w_load[r % 4]
                if r >= 4:
                    sp.wait_ge(w_lo, 2 * (r - 3))
                if kind == "proj":
                    v = raw[:, r % 4, :].rearrange("p (c n) -> p c n", c=NC)
                    for h in range(2):
                        sp.dma_start(v[:, 4 * h:4 * h + 4, :], w_in_v[:, 4 * h:4 * h + 4, j:j + P]).then_inc(done, 16)
                elif kind == "pair":
                    v = raw[:, r % 4, :].rearrange("p (c n) -> p c n", c=NC)
                    for h in range(2):
                        sp.dma_start(v[:, :, HD * h:HD * h + HD],
                                     w_in_v[:, :, j + 4 * HD * h:j + 4 * HD * h + HD]).then_inc(done, 16)
                elif kind in w1_v:
                    v = raw[:, r % 4, :].rearrange("p (c n) -> p c n", c=4)
                    for h in range(2):
                        sp.dma_start(v[:, 2 * h:2 * h + 2, :],
                                     w1_v[kind][:, 4 * j + 2 * h:4 * j + 2 * h + 2, :]).then_inc(done, 16)
                elif kind == "vsg":
                    v = raw[:, r % 4, 0:2 * VSG].rearrange("p (c n) -> p c n", c=2)
                    a, b = COL["v_slc"], COL["v_win"]
                    sp.dma_start(v[:, :, 0:P], w_in_v[:, 2 * j:2 * j + 2, a:a + P]).then_inc(done, 16)
                    sp.dma_start(v[:, :, P:VSG], w_in_v[:, 2 * j:2 * j + 2, b:b + VSG - P]).then_inc(done, 16)
                elif kind == "vb":
                    for h in range(2):
                        sp.dma_start(raw[:, r % 4, S * h:S * h + S],
                                     w_in_v[:, 2 * j + h, COL["v_b"]:COL["v_b"] + S]).then_inc(done, 16)
                else:
                    for h in range(2):
                        row = HD * (j + 4 * h) if j < NSA_PAIRS else P * j + HD * h
                        sp.dma_start(raw[HD * h:HD * h + HD, r % 4, :], w_out[row:row + HD, :]).then_inc(done, 16)

            def swap_halves(n):
                sp.wait_ge(t_evac, t_of[ropes[n]] + 1)
                if n == 0:
                    sp.wait_ge(xs_zero, 1)
                if n >= 2:
                    sp.wait_ge(rope_add, n - 1)
                half = HD // 8
                for base in (0, HD):
                    for a, b in ((base, base + half), (base + half, base)):
                        sp.dma_start(xs[a:a + half, n % 2, :], xf[b:b + half, n % 2, :]).then_inc(swapped[n % 2], 16)

            for r in range(NW):
                if r == 1:
                    sp.wait_ge(x_load[NT - 1], 16)
                if r - 6 in rho_of:
                    swap_halves(rho_of[r - 6])
                load_weights(r)
            sp.wait_ge(w_used, 2 * (NPH + NZ))
            sp.dma_start(gpost, post_g.partition_broadcast(P)).then_inc(g_load, 16)
            sp.wait_ge(pv_done, 4 * NU)
            for t in range(NT):
                sp.dma_start(x_in[:, t, :], x_v[:, t, :]).then_inc(r_load, 16)
            for t in range(NT):
                for h, added in ((0, y_add_g), (1, y_add_v)):
                    sp.wait_ge(added, t + 1)
                    hc = slice(S * h, S * h + S)
                    sp.dma_start(out_v[:, t, hc], y_out[:, t, hc]).then_inc(y_stored, 16)
            sp.wait_ge(y_stored, 32 * NT)

        @block.gpsimd
        def _(pool):
            nc.gpsimd.memset(tok[:, 0], 0.0)
            nc.gpsimd.memset(tok[:, 1], 1.0).then_inc(tok_set, 1)
            for i, pos in enumerate((ck_pos, cv_pos)):
                for h in range(2):
                    pool.dma_start(posr[i][:, HD * h:HD * h + HD], pos).then_inc(k_load, 16)
            w2v_k = ck_w2.rearrange("(j p) n -> p j n", p=P)
            for h in range(2):
                pool.dma_start(w2k[:, :, HD * h:HD * h + HD], w2v_k).then_inc(k_load, 16)
            pool.dma_start(w2v, cv_w2.rearrange("(j p) n -> p j n", p=P)).then_inc(k_load, 16)
            pool.dma_start(cst[:, C_CAUSAL:C_END], consts[:, C_CAUSAL:C_END]).then_inc(t_load, 16)
            nc.gpsimd.memset(zf[:, 1344:2112], 0.0)
            nc.gpsimd.memset(kbd_h[:, :], 0.0)
            nc.gpsimd.memset(kbd_l[:, :], 0.0).then_inc(zeroed, 1)
            nc.gpsimd.memset(gw[:, 2 * NSA_PAIRS:NU, :, :], 1.0).then_inc(zeroed, 1)
            nc.gpsimd.memset(xs[:, :, :], 0.0).then_inc(xs_zero, 1)
            pool.wait_ge(table, 2)
            for n, r in enumerate(ropes):
                pool.wait_ge(t_evac, t_of[r] + 1)
                if n >= 3:
                    pool.wait_ge(rope_lo, n - 2)
                dst = rr[:, n % 2, :] if n else kc_t
                nc.gpsimd.tensor_tensor(dst, xf[:, n % 2, :], cos_t, ALU.mult).then_inc(rope_u, 1)

            def mixed(o):
                mx = mix[:, o % 2, :]
                if o < NSA_PAIRS:
                    pool.wait_ge(o_read, 2 * o + 2)
                    nc.gpsimd.tensor_tensor(mx, mx, zreg[:, o, :], ALU.mult).then_inc(mix_z, 1)
                pool.wait_ge(m_hi, o + 1)
                nc.gpsimd.tensor_tensor(r32(q_l[:, o, :]), mx, q_h[:, o, :], ALU.subtract).then_inc(m_lo, 1)

            def silu(z):
                zt = zreg[:, PAIRS - NZ + z, :]
                pool.wait_ge(t_evac, NPRE + z + 1)
                nc.gpsimd.tensor_tensor(zt, zt, zhalf, ALU.mult).then_inc(z_mul, 1)
                pool.wait_ge(z_mul, z + 1)
                nc.gpsimd.tensor_tensor(zt, zt, zhalf, ALU.add).then_inc(z_silu, 1)

            for U in range(NU):
                if U % 2 == 1 and U // 2 < NZ:
                    silu(U // 2)
                for i in range(3):
                    qt = 3 - i
                    N = P * (qt + 1)
                    pool.wait_ge(w_ready, 4 * U + i + 1)
                    for a in range(2):
                        pa = prob[:, U % 2, a, off(qt):off(qt) + N]
                        last = nc.gpsimd.tensor_tensor(
                            pa, pa, rw[:, U % 2, qt, a:a + 1].to_broadcast([P, N]), ALU.mult)
                    last.then_inc(pn_g, 1)
                if U >= 2 and mixed_after(U - 2) is not None:
                    mixed(mixed_after(U - 2))
            mixed(PAIRS - 2)
            mixed(PAIRS - 1)
            for t in range(NT):
                pool.wait_ge(r_load, 16 * NT)
                pool.wait_ge(y_mul, 2 * t + 1)
                nc.gpsimd.tensor_tensor(y_out[:, t, 0:S], y_out[:, t, 0:S], x_in[:, t, 0:S], ALU.add)\
                    .then_inc(y_add_g, 1)

        @block.scalar
        def _(act):
            act.dma_start(posi, positions.rearrange("b (t p) -> (b t) p", p=P)).then_inc(p_load, 16)
            act.dma_start(cst[:, 0:C_CAUSAL], consts[:, 0:C_CAUSAL]).then_inc(c_load, 16)
            act.dma_start(grow, pre_g.rearrange("(c p) -> c p", p=P)).then_inc(c_load, 16)
            for t in range(NT):
                act.wait_ge(x_load[t], 16)
                if t:
                    act.wait_ge(ssq, t)
                nc.scalar.activation(xjunk, x_in[:, t, :], ACT.Square, accum_out=stat[:, t:t + 1]).then_inc(ssq, 1)
                act.wait_ge(var, t + 1)
                nc.scalar.activation(stat[:, 8 + t:9 + t], stat[:, 4 + t:5 + t], ACT.Sqrt).then_inc(std, 1)

            def split_high(r, which=slice(0, 2)):
                act.wait_ge(w_load[r % 4], 32 * (r // 4 + 1))
                for h, n in list(enumerate(halves(r)))[which]:
                    if r >= 2:
                        act.wait_ge(w_used, 2 * (r - 2) + h + 1)
                    nc.scalar.activation(r32(w_h[:, r % 2, n]), raw[:, r % 4, n], ACT.Copy).then_inc(w_hi, 1)

            split_high(0)
            for c in range(NC):
                act.wait_ge(x_tr, c + 1)
                if c == 0:
                    act.wait_ge(pos_cp, 2)
                nc.scalar.activation(r32(h_h[:, c, :]), ps[:, c, :], ACT.Copy, scale=gpre[:, c:c + 1])\
                    .then_inc(h_hi, 1)
            split_high(1)

            def evacuate(r):
                kind, base, how = tiles[r]
                t = t_of[r]
                act.wait_ge(w_used, 2 * (r + 1))
                bank = ps[:, t % 2 if t < NPRE else 7, :]
                if how == ROPE:
                    n = rho_of[r]
                    if n >= 2:
                        act.wait_ge(rope_add, n - 1)
                    nc.scalar.activation(xf[:, n % 2, :], bank, ACT.Copy).then_inc(t_evac, 1)
                elif how == COPY:
                    nc.scalar.activation(vc_t, bank, ACT.Copy).then_inc(t_evac, 1)
                else:
                    z = t - 16
                    if z == 0:
                        act.wait_ge(c_mm, 2)
                    if z == 1:
                        act.wait_ge(co_mm, 4)
                    if t < NPRE:
                        nc.scalar.activation(zreg[:, z, :], bank, ACT.Silu).then_inc(t_evac, 1)
                    else:
                        if z > PAIRS - NZ:
                            act.wait_ge(z_silu, z - (PAIRS - NZ))
                        nc.scalar.activation(zreg[:, z, :], bank, ACT.Tanh, scale=0.5)
                        nc.scalar.activation(zhalf, bank, ACT.Copy, scale=0.5).then_inc(t_evac, 1)

            def rope_high(n):
                act.wait_ge(rope_add, n + 1)
                nc.scalar.activation(r32(qk_slot(n)[0]), rr[:, n % 2, :], ACT.Copy).then_inc(rope_hi, 1)

            def values(v, r0):
                act.wait_ge(w_used, 2 * (r0 + 4))
                bank = ps[:, 4 + v, :]
                if r0 == R_VSG:
                    nc.scalar.activation(v3[:, 0:4, v, 0, :], bank[:, 0:2 * P].rearrange("p (u d) -> p u d", u=4),
                                         ACT.Copy)
                    nc.scalar.activation(gates[:, v, :], bank[:, 2 * P:VSG], ACT.Copy).then_inc(v_hi, 1)
                else:
                    nc.scalar.activation(v3[:, 4:12, v, 0, :], bank.rearrange("p (u d) -> p u d", u=8),
                                         ACT.Copy).then_inc(v_hi, 1)

            for r in range(NPH):
                split_high(r + 2)
                if r in t_of:
                    evacuate(r)
                if r == 0:
                    act.wait_ge(angle, 1)
                    act.wait_ge(tok_set, 1)
                    for i in range(2):
                        last = nc.scalar.activation(tok[:, i, :, :, 0:NF],
                                                    red[:, i].unsqueeze(2).to_broadcast([P, NT, 2, NF]), ACT.Sin)
                    last.then_inc(table_tok, 1)
                if r == 1:
                    act.wait_ge(table_tr, 1)
                    for i, dst in enumerate((sin_t, cos_t)):
                        nc.scalar.activation(dst, ps[:, 5 + i, :], ACT.Copy).then_inc(table, 1)
                if r in (R_W1K + 6, R_W1V + 6):
                    i = 0 if r == R_W1K + 6 else 1
                    act.wait_ge(w_used, 2 * (r + 1))
                    nc.scalar.activation(h1s[i], ps[0:2 * NB, 3, 0:CH], ACT.Silu).then_inc(h1_silu, 1)
                if rotated_at(r):
                    rope_high(rotated_at(r))
                if r == 1:
                    act.wait_ge(f_built, 1)
                    nc.scalar.activation(r32(f_h[0]), f_tmp, ACT.Copy).then_inc(f_hi_done, 1)
                if r == R_W1K + 4:
                    act.wait_ge(f_built, 2)
                    nc.scalar.activation(r32(f_h[1]), f_tmp, ACT.Copy).then_inc(f_hi_done, 1)
                if r == R_VSG + 2:
                    act.wait_ge(c_mm, 1)
                    act.wait_ge(zeroed, 1)
                    for g in range(2):
                        rows = slice(HD * g, HD * g + HD)
                        last = nc.scalar.activation(r32(kbd_h[rows, CP * g:CP * g + NB]),
                                                    ps[rows, 3, 384 + NB * g:384 + NB * g + NB], ACT.Copy)
                    last.then_inc(c_hi, 1)
                if r in (R_VSG + 3, R_VB + 3):
                    for v in range(NT):
                        values(v, r - 3)
                    if r == R_VSG + 3:
                        act.wait_ge(v_hi, 4)
                        nc.scalar.activation(gates[:, :, :], gates[:, :, :], ACT.Exp, scale=-1.0)\
                            .then_inc(gate_exp, 1)
                if r == R_KB:
                    act.wait_ge(cs_dve, 3)
                    nc.scalar.activation(cs, cs, ACT.Exp, scale=SCALE).then_inc(cs_exp, 1)
                if r == R_KB + 3:
                    for p in range(4):
                        act.wait_ge(cp_tr, p + 1)
                        nc.scalar.activation(pct[0:2 * CP, p, :], ps[0:2 * CP, 4 + p, :], ACT.Copy)\
                            .then_inc(cp_cp, 1)
                if r == R_KB + 4:
                    for p in range(4):
                        act.wait_ge(co_mm, p + 1)
                        nc.scalar.activation(oc[:, p, :], ps[:, 4 + p, :], ACT.Copy).then_inc(co_cp, 1)

            def exps(U, i):
                qt = 3 - i
                N = P * (qt + 1)
                for a in range(2):
                    act.wait_ge(s_masked, 8 * U + 2 * i + a + 1)
                    pa = prob[:, U % 2, a, off(qt):off(qt) + N]
                    nc.scalar.activation(pa, pa, ACT.Exp, bias=nmx[:, U % 2, qt, a:a + 1], scale=-1.0,
                                         accum_out=den[:, U % 2, qt, a:a + 1]).then_inc(p_exp, 1)

            def pt_high(U, i):
                N = P * (i + 1)
                for a in range(2):
                    m = (2 * i + a) % 4
                    act.wait_ge(pt_ready, 8 * U + 2 * i + a + 1)
                    if U:
                        act.wait_ge(pv_done, 4 * U + i - 3)
                    nc.scalar.activation(pt_h[:, a, off(i):off(i) + N], ps[:, 2 + m, 0:N], ACT.Copy).then_inc(pt_hi, 1)

            def mix_high(o):
                if o < NSA_PAIRS:
                    act.wait_ge(mix_z, o + 1)
                else:
                    act.wait_ge(o_read, o + NSA_PAIRS + 1)
                nc.scalar.activation(r32(q_h[:, o, :]), mix[:, o % 2, :], ACT.Copy).then_inc(m_hi, 1)

            for g in range(4):
                exps(0, g)
            evacuate(NPH)
            for g in range(G):
                U, i = g // 4, g % 4
                if U + 1 < NU:
                    exps(U + 1, i)
                pt_high(U, i)
                if g % ZP in (0, 2) and g // ZP < NZ:
                    h = g % ZP // 2
                    split_high(NPH + g // ZP + 2, slice(h, h + 1))
                if g % ZP == ZP - 1 and g // ZP < NZ - 1:
                    evacuate(NPH + g // ZP + 1)
                if i == 3 and U >= 1 and mixed_after(U - 1) is not None:
                    mix_high(mixed_after(U - 1))
            mix_high(PAIRS - 1)
            for r in range(NPH + NZ + 2, NW):
                split_high(r)
            act.wait_ge(std, NT)
            nc.scalar.activation(stat[:, 60:61], stat[:, 8:9], ACT.Sqrt)
            for t in range(NT):
                for h in range(2):
                    act.wait_ge(y_mm, 2 * t + h + 1)
                    last = nc.scalar.activation(junk[:, S * h:S * h + S], ps[:, 2 * t + h, :], ACT.Square,
                                                accum_out=stat[:, 16 + 2 * t + h:17 + 2 * t + h])
                    last.then_inc(y_sq, 1)
                    act.wait_ge(y_sq, 2 * t + h + 1)
                act.wait_ge(y_var, t + 1)
                nc.scalar.activation(stat[:, 32 + t:33 + t], stat[:, 28 + t:29 + t], ACT.Sqrt).then_inc(y_std, 1)

        @block.vector
        def _(dve):
            V = nc.vector
            k = 0

            def link(ins):
                nonlocal k
                k += 1
                ins.then_inc(chain, 1)
                dve.wait_ge(chain, k)

            dve.wait_ge(p_load, 16)
            V.tensor_copy(posf, posi).then_inc(pos_f, 1)
            for t in range(NT):
                dve.wait_ge(ssq, t + 1)
                V.tensor_scalar(stat[:, 4 + t:5 + t], stat[:, t:t + 1], 1.0 / DM, EPS, ALU.mult, ALU.add)\
                    .then_inc(var, 1)
                dve.wait_ge(std, t + 1)
                link(V.reciprocal(stat[:, 12 + t:13 + t], stat[:, 8 + t:9 + t]))
                V.tensor_scalar(x_n[:, t, :], x_in[:, t, :], stat[:, 12 + t:13 + t], None, ALU.mult)\
                    .then_inc(xn_done, 1)
                if t == 0:
                    dve.wait_ge(pos_tr, 1)
                    V.tensor_copy(gpre[:, :], ps[:, 7, 0:NC]).then_inc(pos_cp, 1)
                    V.tensor_copy(stat[:, 48:48 + NT], ps[:, 7, 400:400 + NT]).then_inc(pos_cp, 1)

            def split_low(r, which=slice(0, 2)):
                for h, n in list(enumerate(halves(r)))[which]:
                    dve.wait_ge(w_hi, 2 * r + h + 1)
                    V.tensor_tensor(r32(w_l[:, r % 2, n]), raw[:, r % 4, n], w_h[:, r % 2, n], ALU.subtract)\
                        .then_inc(w_lo, 1)

            split_low(0)
            for c in range(NC):
                dve.wait_ge(h_hi, c + 1)
                V.scalar_tensor_tensor(r32(h_l[:, c, :]), ps[:, c, :], gpre[:, c:c + 1], h_h[:, c, :],
                                       ALU.mult, ALU.subtract).then_inc(h_lo, 1)
            split_low(1)
            dve.wait_ge(pos_cp, 2)
            link(V.tensor_tensor(ang, stat[:, 48:48 + NT].unsqueeze(2).to_broadcast([P, NT, NF]),
                                 inv.unsqueeze(1).to_broadcast([P, NT, NF]), ALU.mult))
            for i in range(2):
                last = V.tensor_scalar(trn[:, i], ang, float(1 / TWO_PI), 0.25 * i, ALU.mult, ALU.add)
            link(last)
            link(V.tensor_scalar(trn, trn, ROUND, None, ALU.add))
            link(V.tensor_scalar(trn, trn, ROUND, None, ALU.subtract))
            both = ang.unsqueeze(1).to_broadcast([P, 2, NT, NF])
            link(V.scalar_tensor_tensor(red, trn, -TP1, both, ALU.mult, ALU.add))
            link(V.scalar_tensor_tensor(red, trn, -TP2, red, ALU.mult, ALU.add))
            link(V.scalar_tensor_tensor(red, trn, -TP3, red, ALU.mult, ALU.add))
            link(V.tensor_scalar(red[:, 1], red[:, 1], float(np.pi / 2), None, ALU.add))
            V.tensor_scalar(red, red, PI_IN, -PI_IN, ALU.min, ALU.max).then_inc(angle, 1)

            def rope(n):
                if n == 0:
                    dve.wait_ge(table, 2)
                dve.wait_ge(swapped[n % 2], 64 * (n // 2 + 1))
                V.tensor_tensor(xs[:, n % 2, :], xs[:, n % 2, :], sin_t, ALU.mult).then_inc(rope_mul, 1)
                dve.wait_ge(rope_mul, n + 1)
                dve.wait_ge(rope_u, n + 1)
                dst = rr[:, n % 2, :] if n else kc_t
                V.tensor_tensor(dst, dst, xs[:, n % 2, :], ALU.add).then_inc(rope_add, 1)
                if n:
                    dve.wait_ge(rope_hi, n)
                    hi, lo = qk_slot(n)
                    V.tensor_tensor(r32(lo), rr[:, n % 2, :], hi, ALU.subtract).then_inc(rope_lo, 1)

            def blocks(i):
                src = (kc_t, vc_t)[i]
                fv = f_tmp.rearrange("p (a j g c) -> p a j g c", a=2, j=8, g=2)
                if i:
                    dve.wait_ge(f_lo_done, 1)
                    dve.wait_ge(t_evac, 2)
                else:
                    dve.wait_ge(rope_add, 1)
                    dve.wait_ge(pos_cp, 4)
                for g in range(2):
                    rows = slice(HD * g, HD * g + HD)
                    sv_ = src[rows, :].rearrange("p (c j t) -> p t j c", j=8, t=2)
                    pv_ = post[i][rows, :].rearrange("p (a j t) -> p a t j", a=2, t=2)
                    for half in range(2):
                        for a in range(2):
                            last = V.tensor_tensor(
                                fv[HD * half:HD * half + HD, a, :, g, :],
                                sv_[:, half, :, a:a + NB],
                                pv_[:, a, half, :].unsqueeze(2).to_broadcast([HD, 8, NB]), ALU.add)
                last.then_inc(f_built, 1)

            def blocks_low(i):
                dve.wait_ge(f_hi_done, i + 1)
                V.tensor_tensor(r32(f_l[i]), f_tmp, f_h[i], ALU.subtract).then_inc(f_lo_done, 1)

            def values_low(v, r0):
                vi = v + (4 if r0 == R_VB else 0)
                n, u0 = (2 * P, 0) if r0 == R_VSG else (S, 4)
                u1 = u0 + n // HD
                rest = vt[:, 0:n].rearrange("p (u d) -> p u d", d=HD)
                dve.wait_ge(v_hi, vi + 1)
                if vi:
                    dve.wait_ge(v_done, vi)
                V.tensor_tensor(rest, ps[:, 4 + v, 0:n].rearrange("p (u d) -> p u d", d=HD),
                                v3[:, u0:u1, v, 0, :], ALU.subtract).then_inc(v_rest, 1)
                dve.wait_ge(v_rest, vi + 1)
                V.tensor_copy(v3[:, u0:u1, v, 1, :], rest).then_inc(v_mid, 1)
                dve.wait_ge(v_mid, vi + 1)
                V.tensor_tensor(v3[:, u0:u1, v, 2, :], rest, v3[:, u0:u1, v, 1, :], ALU.subtract)\
                    .then_inc(v_done, 1)

            for r in range(NPH):
                split_low(r + 2)
                if rotated_at(r) is not None:
                    rope(rotated_at(r))
                if r == 1:
                    dve.wait_ge(pos_tr, 2)
                    for i in range(2):
                        V.tensor_copy(post[i], ps[:, 4, CL * i:CL * (i + 1)]).then_inc(pos_cp, 1)
                if r == R_VSG + 1:
                    dve.wait_ge(h1_tr, 1)
                    V.tensor_copy(h1kt, ps[:, 3, CH:CH + 4 * NB].rearrange("p (j n) -> p j n", j=2)).then_inc(h1_cp, 1)
                if r in (1, R_W1K + 2):
                    blocks(0 if r == 1 else 1)
                if r in (1, R_W1K + 4):
                    blocks_low(0 if r == 1 else 1)
                if r == R_VSG + 2:
                    dve.wait_ge(c_hi, 1)
                    for g in range(2):
                        rows = slice(HD * g, HD * g + HD)
                        last = V.tensor_tensor(r32(kbd_l[rows, CP * g:CP * g + NB]),
                                               ps[rows, 3, 384 + NB * g:384 + NB * g + NB],
                                               kbd_h[rows, CP * g:CP * g + NB], ALU.subtract)
                    last.then_inc(c_lo, 1)
                if r == R_KB:
                    dve.wait_ge(h1_tr, 2)
                    dve.wait_ge(zeroed, 1)
                    for j in range(2):
                        last = V.tensor_copy(h1vt[:, j, :, 0:NB],
                                             ps[:, 3, CH + 2 * NB * j:CH + 2 * NB * (j + 1)]
                                             .rearrange("p (g n) -> p g n", g=2))
                    last.then_inc(h1_cp, 1)
                if r == R_KB + 2:
                    dve.wait_ge(c_mm, 2)
                    for g in range(2):
                        rows = slice(CP * g, CP * g + CP)
                        last = V.tensor_copy(vbd[rows, HD * g:HD * g + HD], ps[rows, 3, 448:512])
                    last.then_inc(c_lo, 1)
                if r in (R_VSG + 3, R_VB + 3):
                    for v in range(NT):
                        values_low(v, r - 3)
                    if r == R_VSG + 3:
                        dve.wait_ge(gate_exp, 1)
                        link(V.tensor_scalar(gates[:, :, :], gates[:, :, :], 1.0, None, ALU.add))
                        link(V.reciprocal(gates[:, :, :], gates[:, :, :]))
                        gv = gates[:, :, :].rearrange("p t (b a q) -> p b a q t", b=3, a=2)
                        for b in range(2):
                            for a in range(2):
                                last = V.tensor_copy(gw[:, b:2 * NSA_PAIRS:2, :, a], gv[:, b + 1, a, :, :])
                        last.then_inc(gates_ready, 1)
                if r == R_KB - 1:
                    dve.wait_ge(cs_mm, 1)
                    dve.wait_ge(t_load, 16)
                    for b in range(2):
                        sc = ps[:, 4 + b, :].rearrange("p (t h c) -> p t h c", t=2, h=8)
                        last = V.tensor_tensor(cs[:, 2 * b:2 * b + 2, :, :], sc,
                                               cadd[:, 2 * b:2 * b + 2, :].unsqueeze(2).to_broadcast([P, 2, 8, CP]),
                                               ALU.add)
                    last.then_inc(cs_dve, 1)
                    dve.wait_ge(cs_dve, 1)
                    csf = cs.rearrange("p t h c -> p (t h) c")
                    V.tensor_reduce(cden[:, 0, :], csf, AX, ALU.max).then_inc(cs_dve, 1)
                    dve.wait_ge(cs_dve, 2)
                    V.tensor_tensor(csf, csf, cden[:, 0, :].unsqueeze(2).to_broadcast([P, NT * 8, CP]),
                                    ALU.subtract).then_inc(cs_dve, 1)
                if r == R_KB:
                    dve.wait_ge(cs_exp, 1)
                    csf = cs.rearrange("p t h c -> p (t h) c")
                    link(V.tensor_tensor(cs, cs, cval.unsqueeze(2).to_broadcast([P, NT, 8, CP]), ALU.mult))
                    link(V.tensor_reduce(cden[:, 0, :], csf, AX, ALU.add))
                if r == R_KB + 1:
                    csf = cs.rearrange("p t h c -> p (t h) c")
                    link(V.tensor_scalar(cden[:, 1, :], cden[:, 0, :], 1e-30, None, ALU.max))
                    link(V.reciprocal(cden[:, 2, :], cden[:, 1, :]))
                    link(V.tensor_tensor(cden[:, 1, :].rearrange("p (t q a) -> p t q a", t=NT, a=2),
                                         cden[:, 2, :].rearrange("p (t q a) -> p t q a", t=NT, a=2),
                                         gates[:, :, 0:8].rearrange("p t (a q) -> p t q a", a=2), ALU.mult))
                    V.tensor_tensor(csf, csf, cden[:, 1, :].unsqueeze(2).to_broadcast([P, NT * 8, CP]),
                                    ALU.mult).then_inc(cs_dve, 1)

            def mask(U, i):
                qt = 3 - i
                N = P * (qt + 1)
                bias = causal if U < 2 * NSA_PAIRS else dilated
                dve.wait_ge(s_ready, 4 * U + i + 1)
                if i == 0 and U >= 2:
                    dve.wait_ge(pt_ready, 8 * (U - 1))
                for a in range(2):
                    V.tensor_tensor_reduce(out=prob[:, U % 2, a, off(qt):off(qt) + N], in0=ps[:, s_bank(U, i, a), 0:N],
                                           in1=bias[:, S - N:S], scale=-SCALE, scalar=BIG, op0=ALU.add,
                                           op1=ALU.min, accum_out=nmx[:, U % 2, qt, a:a + 1]).then_inc(s_masked, 1)

            def weigh(U, i):
                qt = 3 - i
                n = 4 * U + i
                dve.wait_ge(p_exp, 2 * n + 2)
                if i == 0 and U >= 2:
                    dve.wait_ge(pn_g, 3 * (U - 1))
                V.reciprocal(rw[:, U % 2, qt, :], den[:, U % 2, qt, :]).then_inc(p_rec, 1)
                dve.wait_ge(p_rec, n + 1)
                V.tensor_tensor(rw[:, U % 2, qt, :], rw[:, U % 2, qt, :], gw[:, U, qt, :], ALU.mult)\
                    .then_inc(w_ready, 1)
                if qt == 0:
                    dve.wait_ge(w_ready, n + 1)
                    N = P * (qt + 1)
                    for a in range(2):
                        pa = prob[:, U % 2, a, off(qt):off(qt) + N]
                        last = V.tensor_scalar(pa, pa, rw[:, U % 2, qt, a:a + 1], None, ALU.mult)
                    last.then_inc(pn_v, 1)

            def pt_low(U, i):
                N = P * (i + 1)
                for a in range(2):
                    m = (2 * i + a) % 4
                    dve.wait_ge(pt_hi, 8 * U + 2 * i + a + 1)
                    c = slice(off(i), off(i) + N)
                    V.tensor_tensor(pt_l[:, a, c], ps[:, 2 + m, 0:N], pt_h[:, a, c], ALU.subtract)\
                        .then_inc(pt_lo, 1)

            def collect(U):
                dve.wait_ge(pv_done, 4 * U + 4)
                bank = ps[:, 6, :]
                if U < 2 * NSA_PAIRS:
                    p = U // 2
                    mx = mix[:, p % 2, :]
                    if U % 2 == 0:
                        if p >= 2:
                            dve.wait_ge(m_hi, p - 1)
                            dve.wait_ge(m_lo, p - 1)
                        if p == 0:
                            dve.wait_ge(co_cp, 4)
                        V.tensor_tensor(mx, bank, oc[:, p, :], ALU.add).then_inc(o_read, 1)
                    else:
                        dve.wait_ge(o_read, U)
                        V.tensor_tensor(mx, bank, mx, ALU.add).then_inc(o_read, 1)
                else:
                    o = U - NSA_PAIRS
                    dve.wait_ge(m_hi, o - 1)
                    dve.wait_ge(m_lo, o - 1)
                    dve.wait_ge(z_silu, o + 1 - (PAIRS - NZ))
                    V.tensor_tensor(mix[:, o % 2, :], bank, zreg[:, o, :], ALU.mult).then_inc(o_read, 1)

            dve.wait_ge(co_mm, 4)
            dve.wait_ge(zeroed, 2)
            dve.wait_ge(gates_ready, 1)
            for i in range(NT):
                mask(0, i)
                if i:
                    weigh(0, i - 1)
            for g in range(G):
                U, i = g // 4, g % 4
                if i == 2 and U >= 1:
                    collect(U - 1)
                if U + 1 < NU:
                    mask(U + 1, i)
                if g:
                    pt_low((g - 1) // 4, (g - 1) % 4)
                if g + 3 < G:
                    weigh((g + 3) // 4, (g + 3) % 4)
                if g % ZP in (1, 3) and g // ZP < NZ:
                    h = g % ZP // 2
                    split_low(NPH + g // ZP + 2, slice(h, h + 1))
            pt_low(NU - 1, NT - 1)
            collect(NU - 1)
            for r in range(NPH + NZ + 2, NW):
                split_low(r)
            dve.wait_ge(g_load, 16)
            dve.wait_ge(r_load, 16 * NT)
            def y_variance(t):
                dve.wait_ge(y_sq, 2 * t + 2)
                link(V.tensor_tensor(stat[:, 24 + t:25 + t], stat[:, 16 + 2 * t:17 + 2 * t],
                                     stat[:, 17 + 2 * t:18 + 2 * t], ALU.add))
                V.tensor_scalar(stat[:, 28 + t:29 + t], stat[:, 24 + t:25 + t], 1.0 / DM, EPS, ALU.mult, ALU.add)\
                    .then_inc(y_var, 1)

            y_variance(0)
            for t in range(NT):
                dve.wait_ge(y_std, t + 1)
                link(V.reciprocal(stat[:, 36 + t:37 + t], stat[:, 32 + t:33 + t]))
                for h in range(2):
                    V.scalar_tensor_tensor(y_out[:, t, S * h:S * h + S], ps[:, 2 * t + h, :],
                                           stat[:, 36 + t:37 + t], gpost[:, S * h:S * h + S],
                                           ALU.mult, ALU.mult).then_inc(y_mul, 1)
                if t + 1 < NT:
                    y_variance(t + 1)
                dve.wait_ge(y_mul, 2 * t + 2)
                V.tensor_tensor(y_out[:, t, S:DM], y_out[:, t, S:DM], x_in[:, t, S:DM], ALU.add)\
                    .then_inc(y_add_v, 1)

        @block.tensor
        def _(pe):
            T = nc.tensor
            pe.wait_ge(c_load, 32)
            pe.wait_ge(pos_f, 1)
            T.transpose(ps[:, 7, 400:400 + NT], posf, ident[0:NT, 0:NT])
            T.transpose(ps[:, 7, 0:NC], grow, ident[0:NC, 0:NC]).then_inc(pos_tr, 1)
            for t in range(NT):
                pe.wait_ge(xn_done, t + 1)
                for c in range(NC):
                    if t == 0 and c == NC - 1:
                        pe.wait_ge(pos_cp, 2)
                    last = T.transpose(ps[:, c, P * t:P * t + P], x_n[:, t, P * c:P * c + P], ident)
                    if t == NT - 1:
                        last.then_inc(x_tr, 1)

            def three(dst, lh, ll, rh, rl, first, last):
                T.matmul(dst, r32(lh), r32(rh), start=first, stop=False)
                T.matmul(dst, r32(ll), r32(rh), start=False, stop=False)
                return T.matmul(dst, r32(lh), r32(rl), start=False, stop=last)

            def main(r):
                kind, j, how = tiles[r]
                pe.wait_ge(w_lo, 2 * r + (1 if kind in ("proj", "pair", "w1k", "w1v") else 2))
                wh, wl = w_h[:, r % 2, :], w_l[:, r % 2, :]
                if kind in ("proj", "pair"):
                    t = t_of[r]
                    if t >= 2:
                        pe.wait_ge(t_evac, t - 1)
                    for c in range(NC):
                        if t == 0:
                            pe.wait_ge(h_lo, c + 1)
                        if c == NC // 2:
                            last.then_inc(w_used, 1)
                            pe.wait_ge(w_lo, 2 * r + 2)
                        cc = slice(P * c, P * c + P)
                        last = three(ps[:, t % 2, :], wh[:, cc], wl[:, cc], h_h[:, c, :], h_l[:, c, :],
                                     c == 0, c == NC - 1)
                elif kind in ("w1k", "w1v"):
                    i = 0 if kind == "w1k" else 1
                    if j == 0:
                        pe.wait_ge(f_lo_done, i + 1)
                        if i:
                            pe.wait_ge(c_lo, 1)
                    for jj in range(4):
                        if jj == 2:
                            last.then_inc(w_used, 1)
                            pe.wait_ge(w_lo, 2 * r + 2)
                        st = 4 * j + jj
                        fc = slice(2 * NB * st, 2 * NB * (st + 1))
                        wc = slice(CH * jj, CH * jj + CH)
                        last = three(ps[0:2 * NB, 3, 0:CH], f_h[i][:, fc], f_l[i][:, fc], wh[:, wc], wl[:, wc],
                                     st == 0, st == 15)
                elif kind in ("vsg", "vb"):
                    N = VSG if kind == "vsg" else S
                    if kind == "vb" and j == 0:
                        pe.wait_ge(co_cp, 4)
                    for t in range(NT):
                        tc = slice(P * t, P * t + P)
                        for jj in range(2):
                            c = 2 * j + jj
                            wc = slice(N * jj, N * jj + N)
                            last = three(ps[:, 4 + t, 0:N], h_h[:, c, tc], h_l[:, c, tc], wh[:, wc], wl[:, wc],
                                         c == 0, c == NC - 1)
                last.then_inc(w_used, 2 if kind in ("vsg", "vb") else 1)

            for r in range(NPH):
                main(r)
                if r == 1:
                    pe.wait_ge(table_tok, 1)
                    for i in range(2):
                        for t in range(NT):
                            last = T.transpose(ps[:, 5 + i, P * t:P * t + P],
                                               tok[:, i, t].rearrange("p a d -> p (a d)"), ident)
                    last.then_inc(table_tr, 1)
                    pe.wait_ge(k_load, 16 * 7)
                    for i in range(2):
                        last = T.transpose(ps[:, 4, CL * i:CL * (i + 1)], posr[i], ident[0:CL, 0:CL])
                    last.then_inc(pos_tr, 1)
                if r in (R_VSG + 1, R_KB):
                    i = 0 if r == R_VSG + 1 else 1
                    pe.wait_ge(h1_silu, i + 1)
                    for j in range(2):
                        last = T.transpose(ps[:, 3, CH + 2 * NB * j:CH + 2 * NB * (j + 1)],
                                           h1s[i][:, P * j:P * j + P], ident[0:2 * NB, 0:2 * NB])
                    last.then_inc(h1_tr, 1)
                if r == R_VSG + 2:
                    pe.wait_ge(h1_cp, 1)
                    for j in range(2):
                        last = T.matmul(ps[:, 3, 384:384 + 2 * NB], w2k[:, j, :], h1kt[:, j, :],
                                        start=j == 0, stop=j == 1)
                    last.then_inc(c_mm, 1)
                if r == R_KB + 2:
                    pe.wait_ge(h1_cp, 2)
                    for j in range(2):
                        last = T.matmul(ps[0:2 * CP, 3, 448:512], h1vt[:, j, :, :].rearrange("p g n -> p (g n)"),
                                        w2v[:, j, :], start=j == 0, stop=j == 1)
                    last.then_inc(c_mm, 1)
                if r in (R_QB, R_QB + 2, R_QB + 4, R_QB + 6):
                    t = (r - R_QB) // 2
                    if t == 0:
                        pe.wait_ge(v_done, 4)
                        pe.wait_ge(rope_lo, 6)
                    for p in range(4):
                        tc = slice(P * t, P * t + P)
                        o = 256 * (t % 2) + 64 * p
                        last = three(ps[:, 4 + t // 2, o:o + 64], q_h[:, p, tc], q_l[:, p, tc],
                                     kbd_h[:, :], kbd_l[:, :], True, True)
                    if t == NT - 1:
                        last.then_inc(cs_mm, 1)
                if r == R_KB + 3:
                    pe.wait_ge(cs_dve, 4)
                    for p in range(4):
                        for t in range(NT):
                            last = T.transpose(ps[0:2 * CP, 4 + p, P * t:P * t + P],
                                               cs[:, t, 2 * p:2 * p + 2, :].rearrange("p h c -> p (h c)"), ident)
                        last.then_inc(cp_tr, 1)
                if r == R_KB + 4:
                    pe.wait_ge(c_lo, 2)
                    for p in range(4):
                        pe.wait_ge(cp_cp, p + 1)
                        T.matmul(ps[:, 4 + p, :], vbd, pct[0:2 * CP, p, :], start=True, stop=True)\
                            .then_inc(co_mm, 1)

            def scores(U, i):
                qt = 3 - i
                N = max(P * (qt + 1), 2 * P)
                p, kk, _ = unit(U)
                if 4 * U + i >= 1:
                    pe.wait_ge(s_masked, 8 * U + 2 * i - (U > UZ and (U > UZ + 1 or i > 0)))
                if U == UZ + 1 and i == 1:
                    pe.wait_ge(t_evac, len(proj))
                for ql, kr in ((q_h, k_h), (q_l, k_h), (q_h, k_l)):
                    for a in range(2):
                        rows = slice(HD * a, HD * a + HD)
                        last = T.matmul(ps[:, s_bank(U, i, a), 0:N], r32(ql[rows, p, P * qt:P * qt + P]),
                                        r32(kr[rows, kk, 0:N]),
                                        start=ql is q_h and kr is k_h, stop=kr is k_l)
                last.then_inc(s_ready, 1)

            def z_part(z, c):
                r = NPH + z
                if c == 0:
                    pe.wait_ge(w_lo, 2 * r + 1)
                    if z:
                        pe.wait_ge(t_evac, NPRE + z)
                if c == NC // 2:
                    pe.wait_ge(w_lo, 2 * r + 2)
                cc = slice(P * c, P * c + P)
                last = three(ps[:, 7, :], w_h[:, r % 2, cc], w_l[:, r % 2, cc], h_h[:, c, :], h_l[:, c, :],
                             c == 0, c == NC - 1)
                if c in (NC // 2 - 1, NC - 1):
                    last.then_inc(w_used, 1)

            def transposes(U, i):
                kt = 3 - i
                if kt:
                    pe.wait_ge(pn_g, 3 * U + i + 1)
                else:
                    pe.wait_ge(pn_v, U + 1)
                for a in range(2):
                    n = 8 * U + 2 * i + a
                    m = (2 * i + a) % 4
                    if n >= 4:
                        pe.wait_ge(pt_lo, n - 3)
                    for qt in range(kt, NT):
                        src = prob[:, U % 2, a, off(qt) + P * kt:off(qt) + P * kt + P]
                        last = T.transpose(ps[:, 2 + m, P * (qt - kt):P * (qt - kt) + P], src, ident)
                    last.then_inc(pt_ready, 1)

            def outputs(U, i):
                kt = 3 - i
                vu = unit(U)[2]
                pe.wait_ge(pt_lo, 8 * U + 2 * i + 2)
                if i == 0 and U:
                    pe.wait_ge(o_read, U)
                N = P * (i + 1)
                for part, pt in ((0, pt_h), (1, pt_h), (2, pt_h), (0, pt_l), (1, pt_l)):
                    for a in range(2):
                        src = pt[:, a, off(i):off(i) + N]
                        dst = ps[HD * a:HD * a + HD, 6, P * kt:S]
                        first = part == 0 and pt is pt_h
                        for c in ((slice(0, P), slice(P, N)) if first and i else (slice(0, N),)):
                            last = T.matmul(dst[:, c], v3[:, vu + a, kt, part, :], src[:, c],
                                            start=first and i == 0, stop=i == 3 and part == 1 and pt is pt_l)
                last.then_inc(pv_done, 1)

            pe.wait_ge(rope_lo, len(ropes) - 1)
            pe.wait_ge(v_done, 2 * NT)
            for i in range(NT):
                z_part(0, 2 * i)
                if i == 0:
                    pe.wait_ge(t_evac, NPRE)
                scores(0, i)
                z_part(0, 2 * i + 1)
            for g in range(G + 2):
                U, i = g // 4, g % 4
                if U + 1 < NU:
                    scores(U + 1, i)
                if g < ZP * (NZ - 1):
                    z_part(1 + g // ZP, g % ZP)
                if g < G:
                    transposes(U, i)
                if g >= 2:
                    outputs((g - 2) // 4, (g - 2) % 4)

            def project_out(o, t, first, last):
                r = NPH + NZ + o
                tc = slice(P * t, P * t + P)
                for h in range(2):
                    hc = slice(S * h, S * h + S)
                    mm = three(ps[:, 2 * t + h, :], q_h[:, o, tc], q_l[:, o, tc], w_h[:, r % 2, hc],
                               w_l[:, r % 2, hc], first, last)
                    if last:
                        mm.then_inc(y_mm, 1)
                return mm

            def wait_for_pair(o):
                pe.wait_ge(w_lo, 2 * (NPH + NZ + o + 1))
                pe.wait_ge(m_lo, o + 1)

            for o in range(PAIRS - 2):
                wait_for_pair(o)
                for t in range(NT):
                    if o == 0 and t == NT - 1:
                        pe.wait_ge(o_read, NU)
                    last = project_out(o, t, o == 0, False)
                last.then_inc(w_used, 2)
            a, b = PAIRS - 2, PAIRS - 1
            for o, t in ((a, 0), (a, 1), (b, 0), (b, 1), (a, 2), (b, 2), (a, 3), (b, 3)):
                if t == 0:
                    wait_for_pair(o)
                project_out(o, t, False, o == b)


def constants():
    c = np.zeros((P, C_END), np.float32)
    c[:, C_ID:C_ID + P] = np.eye(P)
    half = HD // 8
    powers = np.arange(0, 2 * half, 2, dtype=np.float32) / np.float32(2 * half)
    inv = np.float32(1.0) / (np.float32(500000.0) ** powers)
    c[:, C_INV:C_INV + half] = -inv
    c[:, C_INV + half:C_INV + NF] = inv
    i = np.arange(P)[:, None]
    dist = i + 3 * P - np.arange(S)[None, :]
    c[:, C_CAUSAL:C_CAUSAL + S] = np.where(dist >= 0, 0.0, NEG)
    count = ((dist <= 128).astype(int) + (dist % 4 == 0) + (dist % 16 == 0)) * (dist >= 0)
    c[:, C_DIL:C_DIL + S] = np.where(count > 0, np.log(np.maximum(count, 1)) / SCALE, NEG)
    tok = np.arange(P)[:, None, None] + P * np.arange(NT)[None, :, None]
    blk = np.arange(CP)[None, None, :]
    ok = (blk < NB) & (CS * blk + CL - 1 <= tok)
    c[:, C_CADD:C_CVAL] = np.where(ok, 0.0, NEG).reshape(P, -1)
    c[:, C_CVAL:C_END] = ok.reshape(P, -1)
    return c


def kernel(**inputs):
    import concourse.bacc as _bacc
    from concourse.bass_utils import run_bass_kernel_spmd as _run

    nc = _bacc.Bacc("TRN2", target_bir_lowering=False, num_devices=1)
    arrays, args = {}, []
    names = ["x", "positions", "pre_norm_g", "w_in", "cmp_k_pos", "cmp_k_w1", "cmp_k_w2", "cmp_v_pos", "cmp_v_w1",
             "cmp_v_w2", "w_out", "post_norm_g"]
    for name in names:
        a = np.ascontiguousarray(inputs[name])
        if name not in ("x", "positions"):
            a = a[0]
        arrays[f"in_{name}"] = np.ascontiguousarray(a)
    arrays["in_consts"] = constants()
    for name, a in arrays.items():
        args.append(nc.dram_tensor(name, a.shape, mybir.dt.from_np(a.dtype), kind="ExternalInput").ap())
    args.append(nc.dram_tensor("out_0", (1, S, DM), F32, kind="ExternalOutput").ap())
    hymba_kernel(nc, *args)
    r = _run(nc, [arrays], core_ids=[0])
    return r.results[0]["out_0"]
```
